# Optimizing a Trainium2 kernel written in Bass

```python
import jax, jax.numpy as jnp
from jax import lax
import numpy as np
import math

D_MODEL = 1024
BATCH = 1
SEQ = 512
DEPTH = 2

HEAD_DIM = 64
ROPE_DIM = HEAD_DIM // 4
ROPE_THETA = 500000.0
NORM_EPS = 1e-6
Q_BLOCK = 128
D_FF = 4 * D_MODEL

A_HEADS = 8
A_NOPE = HEAD_DIM - ROPE_DIM
A_KV_RANK = 256
IDX_HEADS = 8
IDX_DIM = 64
TOPK_MAX = 256
B_HEADS = 8
C_HEADS = 16
C_KV_GROUPS = 2
C_HPG = C_HEADS // C_KV_GROUPS
CMP_LEN = 32
CMP_STRIDE = 16
CMP_HIDDEN = 2 * HEAD_DIM
SEL_LEN = 64
SEL_N_MAX = 16
WINDOW = 512
N_BRANCH = 3
FORCE_SCORE = 1e4

AB_WIDTHS = (A_HEADS * HEAD_DIM, A_KV_RANK, ROPE_DIM, IDX_HEADS * IDX_DIM, IDX_DIM, IDX_HEADS,
             B_HEADS * HEAD_DIM, B_HEADS * HEAD_DIM, B_HEADS * HEAD_DIM, B_HEADS)
AB_IN = sum(AB_WIDTHS)
C_WIDTHS = (C_HEADS * HEAD_DIM,) + (C_KV_GROUPS * HEAD_DIM,) * 6 + (C_HEADS * N_BRANCH,)
C_IN = sum(C_WIDTHS)
MIX_WIDTH_AB = (A_HEADS + B_HEADS) * HEAD_DIM
MIX_WIDTH_C = C_HEADS * HEAD_DIM
N_EVEN = (DEPTH + 1) // 2
N_ODD = DEPTH // 2


def rms_norm(x, g):
    xf = x.astype(jnp.float32)
    y = xf * lax.rsqrt(jnp.mean(xf * xf, axis=-1, keepdims=True) + NORM_EPS)
    return (y * g.astype(jnp.float32)).astype(x.dtype)

def rope_tables(seq):
    pos = jnp.arange(seq, dtype=jnp.float32)
    inv = ROPE_THETA ** (-jnp.arange(0, ROPE_DIM, 2, dtype=jnp.float32) / ROPE_DIM)
    ang = pos[:, None] * inv[None, :]
    return jnp.cos(ang), jnp.sin(ang)

def partial_rope(x, cos, sin):
    half = ROPE_DIM // 2
    shp = (1, x.shape[1]) + (1,) * (x.ndim - 3) + (half,)
    c = cos.reshape(shp).astype(x.dtype)
    s = sin.reshape(shp).astype(x.dtype)
    x1, x2, rest = x[..., :half], x[..., half:ROPE_DIM], x[..., ROPE_DIM:]
    return jnp.concatenate([x1 * c - x2 * s, x2 * c + x1 * s, rest], axis=-1)

def masked_softmax(s, mask):
    s = jnp.where(mask, s.astype(jnp.float32), -jnp.inf)
    m = jnp.max(s, axis=-1, keepdims=True)
    m = jnp.where(jnp.isfinite(m), m, 0.0)
    e = jnp.where(mask, jnp.exp(s - m), 0.0)
    return e / jnp.maximum(jnp.sum(e, axis=-1, keepdims=True), 1e-30)

def split_cols(y, widths):
    points, acc = [], 0
    for w in widths[:-1]:
        acc += w
        points.append(acc)
    return jnp.split(y, points, axis=-1)

def to_blocks(a):
    b, s = a.shape[:2]
    return jnp.moveaxis(a.reshape((b, s // Q_BLOCK, Q_BLOCK) + a.shape[2:]), 1, 0)

def from_blocks(a):
    n, b, q = a.shape[:3]
    return jnp.moveaxis(a, 0, 1).reshape((b, n * q) + a.shape[3:])

def dsa_mixer(q, ckv, k_rope, q_idx, k_idx, w_idx, w_uk, w_uv):
    b, s = ckv.shape[:2]
    n_keep = min(TOPK_MAX, s // 4)
    scale = HEAD_DIM ** -0.5
    q_abs = jnp.einsum('bshe,rhe->bshr', q[..., ROPE_DIM:], w_uk)
    q_rot = q[..., :ROPE_DIM]
    w_idx = w_idx * (IDX_HEADS ** -0.5 * IDX_DIM ** -0.5)
    gather = jax.vmap(lambda table, ix: table[ix])
    key_pos = jnp.arange(s)

    def block(args):
        i, qa, qr, qi, wi = args
        t = i * Q_BLOCK + jnp.arange(Q_BLOCK)
        causal = key_pos[None, :] <= t[:, None]
        rel = jax.nn.relu(jnp.einsum('bqhd,bsd->bqhs', qi, k_idx))
        score = jnp.einsum('bqhs,bqh->bqs', rel, wi).astype(jnp.float32)
        score = jnp.where(causal[None], score, -jnp.inf)
        _, idx = lax.top_k(score, n_keep)
        valid = idx <= t[None, :, None]
        c_sel = gather(ckv, idx)
        kr_sel = gather(k_rope, idx)
        logits = (jnp.einsum('bqhr,bqkr->bqhk', qa, c_sel)
                  + jnp.einsum('bqhe,bqke->bqhk', qr, kr_sel)) * scale
        p = masked_softmax(logits, valid[:, :, None, :]).astype(c_sel.dtype)
        return jnp.einsum('bqhk,bqkr->bqhr', p, c_sel)

    nblk = s // Q_BLOCK
    o_lat = from_blocks(lax.map(block, (jnp.arange(nblk), to_blocks(q_abs), to_blocks(q_rot),
                                        to_blocks(q_idx), to_blocks(w_idx))))
    return jnp.einsum('bshr,rhd->bshd', o_lat, w_uv)

def fox_mixer(q, k, v, f_logit):
    b, s = q.shape[:2]
    scale = HEAD_DIM ** -0.5
    cum = lax.cumsum(jax.nn.log_sigmoid(f_logit.astype(jnp.float32)), axis=1)
    cum_k = jnp.transpose(cum, (0, 2, 1))
    key_pos = jnp.arange(s)

    def block(args):
        i, qb, cq = args
        t = i * Q_BLOCK + jnp.arange(Q_BLOCK)
        causal = key_pos[None, :] <= t[:, None]
        logits = (jnp.einsum('bqhd,bshd->bhqs', qb, k).astype(jnp.float32) * scale
                  + jnp.transpose(cq, (0, 2, 1))[..., None] - cum_k[:, :, None, :])
        p = masked_softmax(logits, causal[None, None]).astype(v.dtype)
        return jnp.einsum('bhqs,bshd->bqhd', p, v)

    nblk = s // Q_BLOCK
    return from_blocks(lax.map(block, (jnp.arange(nblk), to_blocks(q), to_blocks(cum))))

def nsa_mixer(q, k_cmp, v_cmp, k_sel, v_sel, k_win, v_win, gate_logit,
              pe_k, pe_v, wk1, wk2, wv1, wv2):
    b, s = q.shape[:2]
    g, d = C_KV_GROUPS, HEAD_DIM
    scale = d ** -0.5
    n_cmp = (s - CMP_LEN) // CMP_STRIDE + 1
    n_selb = s // SEL_LEN
    n_keep = min(SEL_N_MAX, n_selb)
    tok = np.arange(n_cmp)[:, None] * CMP_STRIDE + np.arange(CMP_LEN)[None, :]

    def compress(x, pe, w1, w2):
        xb = x[:, tok] + pe[None, None, :, None, :]
        xb = jnp.transpose(xb, (0, 1, 3, 2, 4)).reshape(b, n_cmp, g, CMP_LEN * d)
        return jax.nn.gelu(xb @ w1) @ w2

    kc = compress(k_cmp, pe_k, wk1, wk2)
    vc = compress(v_cmp, pe_v, wv1, wv2)
    cmp_end = jnp.asarray(tok[:, -1])
    sel_start = np.arange(n_selb) * SEL_LEN
    overlap = ((tok[:, 0][None, :] <= sel_start[:, None] + SEL_LEN - 1)
               & (tok[:, -1][None, :] >= sel_start[:, None]))
    overlap = jnp.asarray(overlap, jnp.float32)
    ks_blk = jnp.transpose(k_sel.reshape(b, n_selb, SEL_LEN, g, d), (0, 3, 1, 2, 4))
    vs_blk = jnp.transpose(v_sel.reshape(b, n_selb, SEL_LEN, g, d), (0, 3, 1, 2, 4))
    kw_pad = jnp.pad(k_win, ((0, 0), (WINDOW, 0), (0, 0), (0, 0)))
    vw_pad = jnp.pad(v_win, ((0, 0), (WINDOW, 0), (0, 0), (0, 0)))
    gather2 = jax.vmap(jax.vmap(lambda table, ix: table[ix]))
    qg = q.reshape(b, s, g, C_HPG, d)
    gates = jax.nn.sigmoid(gate_logit.astype(jnp.float32)).reshape(b, s, g, C_HPG, N_BRANCH)
    blk_ids = jnp.arange(n_selb)

    def block(args):
        i, qb, gb = args
        t = i * Q_BLOCK + jnp.arange(Q_BLOCK)
        s_c = jnp.einsum('bqghd,bngd->bghqn', qb, kc) * scale
        p_c = masked_softmax(s_c, cmp_end[None, :] <= t[:, None])
        o_c = jnp.einsum('bghqn,bngd->bqghd', p_c.astype(vc.dtype), vc)
        imp = jnp.einsum('bghqn,jn->bgqj', p_c, overlap)
        cur = t // SEL_LEN
        forced = ((blk_ids[None, :] == 0) | (blk_ids[None, :] == cur[:, None])
                  | (blk_ids[None, :] == cur[:, None] - 1))
        imp = jnp.where(forced, FORCE_SCORE, imp)
        imp = jnp.where(blk_ids[None, :] * SEL_LEN <= t[:, None], imp, -jnp.inf)
        _, idx = lax.top_k(imp, n_keep)
        k_g = gather2(ks_blk, idx).reshape(b, g, Q_BLOCK, n_keep * SEL_LEN, d)
        v_g = gather2(vs_blk, idx).reshape(b, g, Q_BLOCK, n_keep * SEL_LEN, d)
        tok_pos = (idx[..., None] * SEL_LEN + jnp.arange(SEL_LEN)).reshape(b, g, Q_BLOCK, n_keep * SEL_LEN)
        valid_s = tok_pos <= t[None, None, :, None]
        s_s = jnp.einsum('bqghd,bgqkd->bghqk', qb, k_g) * scale
        p_s = masked_softmax(s_s, valid_s[:, :, None]).astype(v_g.dtype)
        o_s = jnp.einsum('bghqk,bgqkd->bqghd', p_s, v_g)
        start = i * Q_BLOCK
        kw = lax.dynamic_slice_in_dim(kw_pad, start, Q_BLOCK + WINDOW, axis=1)
        vw = lax.dynamic_slice_in_dim(vw_pad, start, Q_BLOCK + WINDOW, axis=1)
        pos = start - WINDOW + jnp.arange(Q_BLOCK + WINDOW)
        valid_w = ((pos[None, :] >= 0) & (pos[None, :] <= t[:, None])
                   & (pos[None, :] > t[:, None] - WINDOW))
        s_w = jnp.einsum('bqghd,bkgd->bghqk', qb, kw) * scale
        p_w = masked_softmax(s_w, valid_w).astype(vw.dtype)
        o_w = jnp.einsum('bghqk,bkgd->bqghd', p_w, vw)
        out = gb[..., 0:1] * o_c + gb[..., 1:2] * o_s + gb[..., 2:3] * o_w
        return out.astype(qb.dtype)

    nblk = s // Q_BLOCK
    o = from_blocks(lax.map(block, (jnp.arange(nblk), to_blocks(qg), to_blocks(gates))))
    return o.reshape(b, s, C_HEADS * d)

def ab_layer(u, w_in, b_forget, kv_norm, w_uk, w_uv, kidx_norm, w_out, cos, sin):
    b, s, _ = u.shape
    aq, ackv, akr, aqi, aki, awi, bq, bk, bv, bf = split_cols(u @ w_in, AB_WIDTHS)
    aq = partial_rope(aq.reshape(b, s, A_HEADS, HEAD_DIM), cos, sin)
    ackv = rms_norm(ackv, kv_norm)
    akr = partial_rope(akr, cos, sin)
    aqi = partial_rope(aqi.reshape(b, s, IDX_HEADS, IDX_DIM), cos, sin)
    aki = partial_rope(rms_norm(aki, kidx_norm), cos, sin)
    o_a = dsa_mixer(aq, ackv, akr, aqi, aki, awi, w_uk, w_uv)
    o_b = fox_mixer(bq.reshape(b, s, B_HEADS, HEAD_DIM), bk.reshape(b, s, B_HEADS, HEAD_DIM),
                    bv.reshape(b, s, B_HEADS, HEAD_DIM), bf + b_forget)
    o = jnp.concatenate([o_a.reshape(b, s, -1), o_b.reshape(b, s, -1)], axis=-1)
    return o @ w_out

def c_layer(u, w_in, b_gate, pe_k, pe_v, wk1, wk2, wv1, wv2, w_out, cos, sin):
    b, s, _ = u.shape
    q, kc, vc, ks, vs, kw, vw, gl = split_cols(u @ w_in, C_WIDTHS)
    kv = lambda a: a.reshape(b, s, C_KV_GROUPS, HEAD_DIM)
    q = partial_rope(q.reshape(b, s, C_HEADS, HEAD_DIM), cos, sin)
    kc = partial_rope(kv(kc), cos, sin)
    ks = partial_rope(kv(ks), cos, sin)
    kw = partial_rope(kv(kw), cos, sin)
    o = nsa_mixer(q, kc, kv(vc), ks, kv(vs), kw, kv(vw), gl + b_gate, pe_k, pe_v, wk1, wk2, wv1, wv2)
    return o @ w_out

def sqrelu_mlp(u, w1, w2):
    return jnp.square(jax.nn.relu(u @ w1)) @ w2

def first_inputs(seed: int = 0) -> dict:
    key = jax.random.key(seed)
    ks = jax.random.split(key, 22)
    nrm = lambda k, shape, fan: jax.random.normal(k, shape, jnp.float32) * (fan ** -0.5)
    gain = lambda k, shape: 1.0 + 0.02 * jax.random.normal(k, shape, jnp.float32)
    return {
        "x": jax.random.normal(ks[0], (BATCH, SEQ, D_MODEL), jnp.float32),
        "attn_norm": gain(ks[1], (DEPTH, D_MODEL)),
        "mlp_norm": gain(ks[2], (DEPTH, D_MODEL)),
        "mlp_w1": nrm(ks[3], (DEPTH, D_MODEL, D_FF), D_MODEL),
        "mlp_w2": nrm(ks[4], (DEPTH, D_FF, D_MODEL), D_FF),
        "ab_w_in": nrm(ks[5], (N_EVEN, D_MODEL, AB_IN), D_MODEL),
        "ab_b_forget": jax.random.uniform(ks[6], (N_EVEN, B_HEADS), jnp.float32, 1.0, 6.0),
        "a_kv_norm": gain(ks[7], (N_EVEN, A_KV_RANK)),
        "a_w_uk": nrm(ks[8], (N_EVEN, A_KV_RANK, A_HEADS, A_NOPE), A_KV_RANK),
        "a_w_uv": nrm(ks[9], (N_EVEN, A_KV_RANK, A_HEADS, HEAD_DIM), A_KV_RANK),
        "a_kidx_norm": gain(ks[10], (N_EVEN, IDX_DIM)),
        "ab_w_out": nrm(ks[11], (N_EVEN, MIX_WIDTH_AB, D_MODEL), MIX_WIDTH_AB),
        "c_w_in": nrm(ks[12], (N_ODD, D_MODEL, C_IN), D_MODEL),
        "c_b_gate": 0.1 * jax.random.normal(ks[13], (N_ODD, C_HEADS * N_BRANCH), jnp.float32),
        "c_pe_k": 0.02 * jax.random.normal(ks[14], (N_ODD, CMP_LEN, HEAD_DIM), jnp.float32),
        "c_pe_v": 0.02 * jax.random.normal(ks[15], (N_ODD, CMP_LEN, HEAD_DIM), jnp.float32),
        "c_cmp_k_w1": nrm(ks[16], (N_ODD, CMP_LEN * HEAD_DIM, CMP_HIDDEN), CMP_LEN * HEAD_DIM),
        "c_cmp_k_w2": nrm(ks[17], (N_ODD, CMP_HIDDEN, HEAD_DIM), CMP_HIDDEN),
        "c_cmp_v_w1": nrm(ks[18], (N_ODD, CMP_LEN * HEAD_DIM, CMP_HIDDEN), CMP_LEN * HEAD_DIM),
        "c_cmp_v_w2": nrm(ks[19], (N_ODD, CMP_HIDDEN, HEAD_DIM), CMP_HIDDEN),
        "c_w_out": nrm(ks[20], (N_ODD, MIX_WIDTH_C, D_MODEL), MIX_WIDTH_C),
        "final_norm": gain(ks[21], (D_MODEL,)),
    }

def first_block(x, attn_norm, mlp_norm, mlp_w1, mlp_w2, ab_w_in, ab_b_forget, a_kv_norm, a_w_uk,
              a_w_uv, a_kidx_norm, ab_w_out, c_w_in, c_b_gate, c_pe_k, c_pe_v, c_cmp_k_w1,
              c_cmp_k_w2, c_cmp_v_w1, c_cmp_v_w2, c_w_out, final_norm):
    cos, sin = rope_tables(x.shape[1])
    h = x
    for layer in range(DEPTH):
        u = rms_norm(h, attn_norm[layer])
        if layer % 2 == 0:
            j = layer // 2
            h = h + ab_layer(u, ab_w_in[j], ab_b_forget[j], a_kv_norm[j], a_w_uk[j], a_w_uv[j],
                             a_kidx_norm[j], ab_w_out[j], cos, sin)
        else:
            j = layer // 2
            h = h + c_layer(u, c_w_in[j], c_b_gate[j], c_pe_k[j], c_pe_v[j], c_cmp_k_w1[j],
                            c_cmp_k_w2[j], c_cmp_v_w1[j], c_cmp_v_w2[j], c_w_out[j], cos, sin)
        h = h + sqrelu_mlp(rms_norm(h, mlp_norm[layer]), mlp_w1[layer], mlp_w2[layer])
    return rms_norm(h, final_norm)


DEPTH_2 = 1

CHUNK = 64
DA_HEADS = 4
DA_HEAD_DIM = 64
DA_WIDTH = DA_HEADS * 2 * DA_HEAD_DIM
SB_HEADS = 8
SB_HEAD_DIM = 64
SB_WIDTH = SB_HEADS * SB_HEAD_DIM
MIX_WIDTH = DA_WIDTH + SB_WIDTH
IN_WIDTH = 3 * DA_WIDTH + 3 * SB_WIDTH
REL_BUCKETS = 32
REL_MAX_DIST = 128
N_GROUPS = 4
EXPERTS_PER_GROUP = 8
N_EXPERTS = N_GROUPS * EXPERTS_PER_GROUP
TOP_K = 2
EXPERT_HIDDEN = 512
MOE_BLOCK = 256
EPS = 1e-6


def rms_norm_2(x, g):
    xf = x.astype(jnp.float32)
    y = xf * lax.rsqrt(jnp.mean(xf * xf, axis=-1, keepdims=True) + EPS)
    return (y * g.astype(jnp.float32)).astype(x.dtype)

def rel_bucket(rel):
    nb = REL_BUCKETS // 2
    max_exact = nb // 2
    base = jnp.where(rel > 0, nb, 0)
    n = jnp.abs(rel)
    nf = jnp.maximum(n, 1).astype(jnp.float32)
    large = max_exact + (jnp.log(nf / max_exact) / math.log(REL_MAX_DIST / max_exact)
                         * (nb - max_exact)).astype(jnp.int32)
    large = jnp.minimum(large, nb - 1)
    return base + jnp.where(n < max_exact, n, large)

def to_blocks_2(t):
    b, h, s, d = t.shape
    return jnp.transpose(t.reshape(b, h, s // Q_BLOCK, Q_BLOCK, d), (2, 0, 1, 3, 4))

def from_blocks_2(t):
    nblk, b, h, qb, d = t.shape
    return jnp.transpose(t, (1, 2, 0, 3, 4)).reshape(b, h, nblk * qb, d)

def diff_attention(q1, q2, k1, k2, v, rel_bias, lam):
    s_len = q1.shape[2]
    scale = q1.shape[-1] ** -0.5
    pos_k = jnp.arange(s_len, dtype=jnp.int32)

    def block(args):
        i, q1b, q2b = args
        pos_q = i * Q_BLOCK + jnp.arange(Q_BLOCK, dtype=jnp.int32)
        mask = (pos_k[None, :] // CHUNK) <= (pos_q[:, None] // CHUNK)
        bias = rel_bias[rel_bucket(pos_k[None, :] - pos_q[:, None])]
        bias = jnp.transpose(bias, (2, 0, 1)).astype(jnp.float32)

        def probs(qb, k):
            s = jnp.einsum('bhqd,bhkd->bhqk', qb, k).astype(jnp.float32) * scale + bias
            return jax.nn.softmax(jnp.where(mask, s, -jnp.inf), axis=-1)

        w = probs(q1b, k1) - lam * probs(q2b, k2)
        return jnp.einsum('bhqk,bhkd->bhqd', w.astype(v.dtype), v)

    nblk = s_len // Q_BLOCK
    out = lax.map(block, (jnp.arange(nblk, dtype=jnp.int32), to_blocks_2(q1), to_blocks_2(q2)))
    return from_blocks_2(out)

def stick_breaking(q, k, v):
    s_len = q.shape[2]
    scale = q.shape[-1] ** -0.5
    pos_k = jnp.arange(s_len, dtype=jnp.int32)

    def block(args):
        i, qb = args
        pos_q = i * Q_BLOCK + jnp.arange(Q_BLOCK, dtype=jnp.int32)
        causal = pos_k[None, :] < pos_q[:, None]
        z = jnp.einsum('bhqd,bhkd->bhqk', qb, k).astype(jnp.float32) * scale
        log_1m = jnp.where(causal, jax.nn.log_sigmoid(-z), 0.0)
        between = lax.cumsum(log_1m, axis=3, reverse=True) - log_1m
        a = jnp.where(causal, jnp.exp(jax.nn.log_sigmoid(z) + between), 0.0)
        return jnp.einsum('bhqk,bhkd->bhqd', a.astype(v.dtype), v)

    nblk = s_len // Q_BLOCK
    out = lax.map(block, (jnp.arange(nblk, dtype=jnp.int32), to_blocks_2(q)))
    return from_blocks_2(out)

def hier_moe(h, wg, bg, we, be, w1, w3, w2):
    bsz, s_len, d = h.shape
    n = bsz * s_len
    hf = h.reshape(n, d)
    pg = jax.nn.softmax((hf @ wg + bg).astype(jnp.float32), axis=-1)
    gsel = jnp.argmax(pg, axis=-1).astype(jnp.int32)
    pg_sel = jnp.max(pg, axis=-1)
    le = (hf @ we + be).astype(jnp.float32).reshape(n, N_GROUPS, EXPERTS_PER_GROUP)
    le = jnp.take_along_axis(le, gsel[:, None, None], axis=1)[:, 0]
    p_top, e_loc = lax.top_k(jax.nn.softmax(le, axis=-1), TOP_K)
    gate = pg_sel[:, None] * p_top / jnp.sum(p_top, axis=-1, keepdims=True)

    eid = (gsel[:, None] * EXPERTS_PER_GROUP + e_loc.astype(jnp.int32)).reshape(-1)
    tok = jnp.repeat(jnp.arange(n, dtype=jnp.int32), TOP_K)
    gflat = gate.reshape(-1)
    order = jnp.argsort(eid)
    s_eid, s_tok, s_gate = eid[order], tok[order], gflat[order]
    counts = jnp.zeros((N_EXPERTS,), jnp.int32).at[eid].add(1)
    starts = jnp.cumsum(counts) - counts
    padded = (counts + MOE_BLOCK - 1) // MOE_BLOCK * MOE_BLOCK
    pad_ends = jnp.cumsum(padded)
    pad_starts = pad_ends - padded
    dest = pad_starts[s_eid] + (jnp.arange(n * TOP_K, dtype=jnp.int32) - starts[s_eid])
    cap = n * TOP_K + N_EXPERTS * MOE_BLOCK
    tok_buf = jnp.full((cap,), n, jnp.int32).at[dest].set(s_tok)
    gate_buf = jnp.zeros((cap,), jnp.float32).at[dest].set(s_gate)
    nb = cap // MOE_BLOCK
    blk_e = jnp.minimum(jnp.searchsorted(pad_ends, jnp.arange(nb, dtype=jnp.int32) * MOE_BLOCK,
                                         side='right'), N_EXPERTS - 1).astype(jnp.int32)
    h_pad = jnp.concatenate([hf, jnp.zeros((1, d), hf.dtype)], axis=0)
    xs = h_pad[tok_buf].reshape(nb, MOE_BLOCK, d)

    def expert_block(args):
        xb, e = args
        return (jax.nn.silu(xb @ w1[e]) * (xb @ w3[e])) @ w2[e]

    ys = lax.map(expert_block, (xs, blk_e)).reshape(cap, d)
    ys = ys * gate_buf[:, None].astype(ys.dtype)
    out = jnp.zeros((n + 1, d), ys.dtype).at[tok_buf].add(ys)[:n]
    return out.reshape(bsz, s_len, d)

def second_inputs(seed: int = 0) -> dict:
    key = jax.random.key(seed)
    ks = jax.random.split(key, 24)
    f32 = jnp.float32
    nrm = lambda k, shape, s: jax.random.normal(k, shape, f32) * s
    gain = lambda k, shape: 1.0 + 0.02 * jax.random.normal(k, shape, f32)
    return {
        "x": jax.random.normal(ks[0], (BATCH, SEQ, D_MODEL), f32),
        "g_attn": gain(ks[1], (DEPTH_2, D_MODEL)),
        "w_in": nrm(ks[2], (DEPTH_2, D_MODEL, IN_WIDTH), D_MODEL ** -0.5),
        "qn_g": gain(ks[3], (DEPTH_2, DA_HEAD_DIM)),
        "kn_g": gain(ks[4], (DEPTH_2, DA_HEAD_DIM)),
        "lam_q1": nrm(ks[5], (DEPTH_2, DA_HEAD_DIM), 0.1),
        "lam_k1": nrm(ks[6], (DEPTH_2, DA_HEAD_DIM), 0.1),
        "lam_q2": nrm(ks[7], (DEPTH_2, DA_HEAD_DIM), 0.1),
        "lam_k2": nrm(ks[8], (DEPTH_2, DA_HEAD_DIM), 0.1),
        "subln_g": gain(ks[9], (DEPTH_2, 2 * DA_HEAD_DIM)),
        "sb_out_g": gain(ks[10], (DEPTH_2, SB_HEAD_DIM)),
        "rel_bias": nrm(ks[11], (REL_BUCKETS, DA_HEADS), 0.5),
        "w_o": nrm(ks[12], (DEPTH_2, MIX_WIDTH, D_MODEL), MIX_WIDTH ** -0.5),
        "g_ffn": gain(ks[13], (DEPTH_2, D_MODEL)),
        "w_router_g": nrm(ks[14], (DEPTH_2, D_MODEL, N_GROUPS), D_MODEL ** -0.5),
        "b_router_g": nrm(ks[15], (DEPTH_2, N_GROUPS), 0.01),
        "w_router_e": nrm(ks[16], (DEPTH_2, D_MODEL, N_EXPERTS), D_MODEL ** -0.5),
        "b_router_e": nrm(ks[17], (DEPTH_2, N_EXPERTS), 0.01),
        "w1": nrm(ks[18], (DEPTH_2, N_EXPERTS, D_MODEL, EXPERT_HIDDEN), D_MODEL ** -0.5),
        "w3": nrm(ks[19], (DEPTH_2, N_EXPERTS, D_MODEL, EXPERT_HIDDEN), D_MODEL ** -0.5),
        "w2": nrm(ks[20], (DEPTH_2, N_EXPERTS, EXPERT_HIDDEN, D_MODEL), EXPERT_HIDDEN ** -0.5),
    }

def second_block(x, g_attn, w_in, qn_g, kn_g, lam_q1, lam_k1, lam_q2, lam_k2, subln_g,
              sb_out_g, rel_bias, w_o, g_ffn, w_router_g, b_router_g, w_router_e,
              b_router_e, w1, w3, w2):
    bsz, s_len, _ = x.shape
    cut = np.cumsum([DA_WIDTH, DA_WIDTH, DA_WIDTH, SB_WIDTH, SB_WIDTH]).tolist()
    for l in range(DEPTH_2):
        lambda_init = 0.8 - 0.6 * math.exp(-0.3 * l)
        h = rms_norm_2(x, g_attn[l])
        proj = h @ w_in[l]
        dq, dk, dv, sq, sk, sv = jnp.split(proj, cut, axis=-1)

        dq = jnp.transpose(dq.reshape(bsz, s_len, DA_HEADS, 2, DA_HEAD_DIM), (3, 0, 2, 1, 4))
        dk = jnp.transpose(dk.reshape(bsz, s_len, DA_HEADS, 2, DA_HEAD_DIM), (3, 0, 2, 1, 4))
        dq = rms_norm_2(dq, qn_g[l])
        dk = rms_norm_2(dk, kn_g[l])
        dv = jnp.transpose(dv.reshape(bsz, s_len, DA_HEADS, 2 * DA_HEAD_DIM), (0, 2, 1, 3))
        lam = (jnp.exp(jnp.sum(lam_q1[l] * lam_k1[l]).astype(jnp.float32))
               - jnp.exp(jnp.sum(lam_q2[l] * lam_k2[l]).astype(jnp.float32)) + lambda_init)
        o_da = diff_attention(dq[0], dq[1], dk[0], dk[1], dv, rel_bias, lam)
        o_da = rms_norm_2(o_da, subln_g[l]) * (1.0 - lambda_init)
        o_da = jnp.transpose(o_da, (0, 2, 1, 3)).reshape(bsz, s_len, DA_WIDTH)

        to_heads = lambda t: jnp.transpose(t.reshape(bsz, s_len, SB_HEADS, SB_HEAD_DIM), (0, 2, 1, 3))
        o_sb = stick_breaking(to_heads(sq), to_heads(sk), to_heads(sv))
        o_sb = rms_norm_2(o_sb, sb_out_g[l])
        o_sb = jnp.transpose(o_sb, (0, 2, 1, 3)).reshape(bsz, s_len, SB_WIDTH)

        x = x + jnp.concatenate([o_da, o_sb], axis=-1) @ w_o[l]

        h2 = rms_norm_2(x, g_ffn[l])
        x = x + hier_moe(h2, w_router_g[l], b_router_g[l], w_router_e[l], b_router_e[l],
                         w1[l], w3[l], w2[l])
    return x


def setup_inputs(seed=0):
    out = dict(first_inputs(seed))
    for name, value in second_inputs(seed + 1).items():
        if name != "x":
            out[name + "_2"] = value
    return out


def reference(
    x, attn_norm, mlp_norm, mlp_w1, mlp_w2, ab_w_in, ab_b_forget, a_kv_norm, a_w_uk, a_w_uv,
    a_kidx_norm, ab_w_out, c_w_in, c_b_gate, c_pe_k, c_pe_v, c_cmp_k_w1, c_cmp_k_w2, c_cmp_v_w1,
    c_cmp_v_w2, c_w_out, final_norm, g_attn_2, w_in_2, qn_g_2, kn_g_2, lam_q1_2, lam_k1_2,
    lam_q2_2, lam_k2_2, subln_g_2, sb_out_g_2, rel_bias_2, w_o_2, g_ffn_2, w_router_g_2,
    b_router_g_2, w_router_e_2, b_router_e_2, w1_2, w3_2, w2_2,
):
    x = first_block(
        x, attn_norm, mlp_norm, mlp_w1, mlp_w2, ab_w_in, ab_b_forget, a_kv_norm, a_w_uk, a_w_uv,
        a_kidx_norm, ab_w_out, c_w_in, c_b_gate, c_pe_k, c_pe_v, c_cmp_k_w1, c_cmp_k_w2,
        c_cmp_v_w1, c_cmp_v_w2, c_w_out, final_norm,
    )
    return second_block(
        x, g_attn_2, w_in_2, qn_g_2, kn_g_2, lam_q1_2, lam_k1_2, lam_q2_2, lam_k2_2, subln_g_2,
        sb_out_g_2, rel_bias_2, w_o_2, g_ffn_2, w_router_g_2, b_router_g_2, w_router_e_2,
        b_router_e_2, w1_2, w3_2, w2_2,
    )


_drawn_inputs = setup_inputs


def setup_inputs(seed=0):
    import zlib

    import numpy as np

    out = dict(_drawn_inputs(seed))
    spreads = {}
    factors = {'a_kv_norm': 5.487,
     'a_kidx_norm': 2.954,
     'c_pe_k': 25.96,
     'c_pe_v': 5.017,
     'qn_g_2': 8.0,
     'kn_g_2': 5.425,
     'lam_q1_2': 5.761,
     'lam_k1_2': 5.164,
     'lam_q2_2': 10.753,
     'lam_k2_2': 2.804,
     'subln_g_2': 15.058,
     'sb_out_g_2': 13.511,
     'b_router_g_2': 21.704,
     'b_router_e_2': 23.264,
     'g_ffn_2': 5.74}
    for name, (base, spread) in spreads.items():
        noise = np.random.default_rng([zlib.crc32(name.encode()), seed]).standard_normal(out[name].shape)
        drawn = base * np.exp(spread * noise) if base else spread * noise
        out[name] = __import__('jax').numpy.asarray(drawn.astype(out[name].dtype))
    for name, factor in factors.items():
        out[name] = (out[name] * factor).astype(out[name].dtype)
    return out
```

```python
from contextlib import ExitStack

import numpy as np

import concourse.bass as bass
from concourse import mybir
from concourse.alu_op_type import AluOpType as ALU

F32 = mybir.dt.float32
I32 = mybir.dt.int32
U32 = mybir.dt.uint32
ACT = mybir.ActivationFunctionType
AX = mybir.AxisListType

P = 128
T = 512
D = 1024
KT = D // P
NB = T // P
D_FF = 4096
FT = D_FF // P
EPS = 1e-6
NEG = -1e30
TAKEN = -3e38
RING = 8
HD = 64
SCALE = HD ** -0.5
ROPE = 16
TOPK = 128
N_CMP, CMP_LEN, CMP_STRIDE = 31, 32, 16
NE, NG, EPG = 32, 4, 8
EH = 512
CAP = 128
SETS = 4
BUCKETS = 32
LV = 640
LAMBDA_INIT = 0.8 - 0.6

N_AB, N_C, N_2, N_O = 24, 16, 24, 8
CH_AB = 0
CH_ABO = CH_AB + N_AB
CH_M0 = CH_ABO + N_O
CH_C = CH_M0 + 2 * FT
CH_CO = CH_C + N_C
CH_M1 = CH_CO + N_O
CH_2 = CH_M1 + 2 * FT
CH_2O = CH_2 + N_2
N_CH = CH_2O + N_O


def shape_constants():
    p = np.arange(P)
    f = np.float32
    c = {}
    c["ident"] = np.eye(P)
    c["ones"] = np.ones((P, P))
    c["pair_ones"] = (p[:, None] // HD == p[None, :] // HD)
    swap = np.zeros((P, P))
    for r in range(P):
        if r % HD < ROPE // 2:
            swap[r + ROPE // 2, r] = -1.0
        elif r % HD < ROPE:
            swap[r - ROPE // 2, r] = 1.0
    c["swap"] = swap
    sel = np.zeros((P, P))
    for r in range(ROPE):
        sel[HD + r, r] = sel[HD + r, HD + r] = 1.0
    c["sel_rope"] = sel
    dup = np.zeros((P, P))
    for r in range(HD):
        dup[r, r] = dup[r, HD + r] = 1.0
    c["dup"] = dup
    inv = (f(500000.0) ** (-np.arange(0, ROPE, 2, dtype=f) / f(ROPE))).astype(f)
    ang = np.arange(T, dtype=f)[:, None] * inv[None, :]
    cos, sin = np.cos(ang).T, np.sin(ang).T
    rc, rs = np.ones((P, T)), np.zeros((P, T))
    for r in range(P):
        if r % HD < ROPE:
            rc[r], rs[r] = cos[r % HD % (ROPE // 2)], sin[r % HD % (ROPE // 2)]
    c["rope_c"], c["rope_s"] = rc, rs
    c["rope_cq"], c["rope_sq"] = rc * SCALE, rs * SCALE
    k = np.arange(T)[None, :] - (T - P)
    c["causal"] = np.where(k <= p[:, None], 0.0, NEG)
    c["chunked"] = np.where(k // HD <= p[:, None] // HD, 0.0, NEG)
    c["strict"] = np.where(p[:, None] < p[None, :], 0.0, NEG)
    c["tri_from"] = (p[:, None] >= p[None, :])
    c["tri_before"] = (p[:, None] < p[None, :])
    n = np.arange(32)
    t = np.arange(NB)[None, :, None] * P + p[:, None, None]
    ok = (n[None, None, :] < N_CMP) & (n[None, None, :] * CMP_STRIDE + CMP_LEN - 1 <= t)
    ok = np.repeat(ok[:, :, None, :], 2, axis=2)
    c["cmp_add"] = np.where(ok, 0.0, NEG).reshape(P, -1)
    c["cmp_one"] = ok.reshape(P, -1)
    rel = np.arange(LV) - (T - 1)
    half, exact = BUCKETS // 2, BUCKETS // 4
    m = np.abs(rel)
    mf = np.maximum(m, 1).astype(f)
    large = exact + (np.log(mf / f(exact)) / f(np.log(128 / exact)) * f(half - exact)).astype(np.int32)
    bucket = np.where(rel > 0, half, 0) + np.where(m < exact, m, np.minimum(large, half - 1))
    oh = np.zeros((P, LV))
    oh[bucket, np.arange(LV)] = 1.0
    c["buckets"] = oh
    c["iota"] = np.broadcast_to(np.arange(T), (P, T))
    c["rev8"] = np.broadcast_to(8.0 - np.arange(8), (P, 8))
    c["token"] = np.arange(NB)[None, :] * P + p[:, None]
    c["slot"] = p[:, None]
    return {n: np.ascontiguousarray(a, dtype=f) for n, a in c.items()}


class Packed:

    def __init__(self, parts):
        self.at, w = {}, 0
        for name, a in parts.items():
            self.at[name] = (w, a.shape[1])
            w += a.shape[1]
        self.width = w
        self.array = np.concatenate(list(parts.values()), axis=1)

    def view(self, ap, name):
        o, w = self.at[name]
        return ap[:, o:o + w]


def chunks(w):
    k, n = w.shape
    a = w.reshape(k // D, KT, P, n // P, P)
    return a.transpose(3, 0, 2, 1, 4).reshape(-1, P, KT * P)


def columns(w, cols):
    out = np.zeros((w.shape[0], len(cols)), w.dtype)
    cols = np.asarray(cols)
    out[:, cols >= 0] = w[:, cols[cols >= 0]]
    return out


def lay_out(i):
    a = {}
    ab, cw, w2 = i["ab_w_in"][0], i["c_w_in"][0], i["w_in_2"][0]
    r = lambda o, n: list(range(o, o + n))
    pad = lambda n: [-1] * n
    aq, ckv, akr, aqi, aki, awi, bq, bk, bv, bf = np.cumsum([0, 512, 256, 16, 512, 64, 8, 512, 512, 512])
    cols = (r(aq, 512) + r(aqi, 512) + r(bq, 512) + r(bk, 512) + r(ckv, 256)
            + r(aki, 64) + r(akr, 16) + pad(48) + r(bf, 8) + pad(24) + r(awi, 8) + pad(88) + r(bv, 512))
    s_ab = chunks(columns(ab, cols))
    heads = [h for m in range(8) for h in (m, m + 8)]
    q_cols = [h * HD + d for h in heads for d in range(HD)]
    o = [D + 128 * j for j in range(7)]
    gate_cols = [o[6] + h * 3 + b for h in heads for b in range(3)]
    cols = (q_cols + r(o[0], 128) + r(o[2], 128) + r(o[4], 128) + r(o[1], 128) + r(o[3], 128) + r(o[5], 128)
            + gate_cols + pad(80) + pad(128))
    s_c = chunks(columns(cw, cols))
    ml = lambda l: [chunks(i["mlp_w1"][l]), chunks(i["mlp_w2"][l])]
    a["dense"] = np.concatenate([s_ab, chunks(i["ab_w_out"][0])] + ml(0)
                                + [s_c, chunks(i["c_w_out"][0][q_cols])] + ml(1)
                                + [chunks(w2), chunks(i["w_o_2"][0])])
    a["xT"] = i["x"][0].T.reshape(KT, P, T).transpose(1, 0, 2)
    tiles = lambda w: w.reshape(-1, P, w.shape[1]).transpose(1, 0, 2)
    uk = i["a_w_uk"][0]
    ukp = np.zeros((256, 8, HD), np.float32)
    ukp[:, :, ROPE:] = uk
    a["w_uk"] = tiles(ukp.reshape(256, 512))
    a["w_uv"] = tiles(i["a_w_uv"][0].reshape(256, 512))
    for n in "kv":
        w = i[f"c_cmp_{n}_w1"][0].reshape(CMP_LEN, HD, P).transpose(1, 0, 2)
        a[f"cmp_{n}1"] = np.concatenate([w, w], 0)
    k2 = np.zeros((P, 2, P), np.float32)
    k2[:, 0, :HD] = k2[:, 1, HD:] = i["c_cmp_k_w2"][0]
    a["cmp_k2"] = k2
    a["cmp_v2"] = i["c_cmp_v_w2"][0]
    a["router"] = tiles(np.concatenate([i["w_router_g_2"][0], i["w_router_e_2"][0]], 1))
    e1 = lambda w: w.reshape(NE, KT, P, EH).transpose(0, 2, 1, 3).reshape(NE, P, KT * EH)
    a["e1"], a["e3"] = e1(i["w1_2"][0]), e1(i["w3_2"][0])
    a["e2"] = i["w2_2"][0].reshape(NE, EH // P, P, D).transpose(0, 2, 1, 3).reshape(NE, P, -1)
    col = lambda v: v.reshape(-1, P).T
    row = lambda v: np.broadcast_to(v.reshape(1, -1), (P, v.size))
    short = lambda v: np.concatenate([v.reshape(-1, 1), np.zeros((P - v.size, 1), np.float32)], 0)
    twice = lambda v: np.concatenate([v, v], 0)
    rb = np.zeros((P, NG, P), np.float32)
    rb[:BUCKETS] = np.broadcast_to(i["rel_bias_2"][:, :, None], (BUCKETS, 4, P))
    vecs = {
        "g_a0": col(i["attn_norm"][0]), "g_a1": col(i["attn_norm"][1]), "g_m0": col(i["mlp_norm"][0]),
        "g_m1": col(i["mlp_norm"][1]), "g_fin": col(i["final_norm"]), "g_a2": col(i["g_attn_2"][0]),
        "g_ffn": col(i["g_ffn_2"][0]), "g_kv": col(i["a_kv_norm"][0]), "g_ki": short(i["a_kidx_norm"][0]),
        "b_f": short(i["ab_b_forget"][0]), "g_qn": twice(i["qn_g_2"][0][:, None]),
        "g_kn": twice(i["kn_g_2"][0][:, None]), "subln": row(i["subln_g_2"][0]), "sb_g": row(i["sb_out_g_2"][0]),
        "b_gate": row(i["c_b_gate"][0].reshape(16, 3)[heads]),
        "b_router": row(np.concatenate([i["b_router_g_2"][0], i["b_router_e_2"][0]])),
        "lam": row(np.concatenate([i[f"lam_{n}_2"][0] for n in ("q1", "q2", "k1", "k2")])),
        "rel": rb.reshape(P, -1), "pe_k": twice(i["c_pe_k"][0].T), "pe_v": twice(i["c_pe_v"][0].T),
    }
    return a, Packed(vecs)


class Engine:

    def __init__(self, eng, sem):
        self.eng, self.sem, self.n = eng, sem, 0

    def done(self, ins):
        ins.then_inc(self.sem, 1)
        self.n += 1
        return self.sem, self.n

    def wait(self, *ticks):
        for t in ticks:
            if t is not None:
                self.eng.wait_ge(*t)


class Landing:

    def __init__(self, ap, sem):
        self.ap, self.sem = ap, sem

    def load(self, by, src, *released, dst=None):
        by.wait(*released)
        by.eng.dma_start(self.ap if dst is None else dst, src).then_inc(self.sem, 16)

    def wait(self, reader):
        reader.eng.wait_ge(self.sem, 16)
        reader.eng.sem_clear(self.sem)


class Events(dict):

    def __missing__(self, name):
        return None


class Core:

    def __init__(self):
        self.ev, self.names = Events(), 0




def program(nc, t, cpack, vpack, out, upto=None):
    core = Core()
    core.nc, core.t, core.cpack, core.vpack, core.out = nc, t, cpack, vpack, out
    with ExitStack() as stack:
        core.stack = stack
        begin(core)
        layer_ab(core)
        if upto != "a0":
            mlp(core, CH_M0, "g_m0")
        if upto not in ("a0", "m0"):
            layer_c(core)
        if upto not in ("a0", "m0", "a1"):
            mlp(core, CH_M1, "g_m1")
            norm(core, "g_fin", core.x)
        if upto not in ("a0", "m0", "a1", "fn"):
            layer_2(core)
        if upto is not None:
            dump_x(core)
            return
        moe(core)


def sb(core, name, shape, dt=F32, stack=None):
    core.names += 1
    return (stack or core.stack).enter_context(core.nc.sbuf_tensor(f"{name}_{core.names}", shape, dt)).ap()


def sem(core, name):
    return core.stack.enter_context(core.nc.semaphore(name))


def landing(core, name, shape, stack=None, dt=F32):
    return Landing(sb(core, name, shape, dt, stack), sem(core, "landed_" + name))


def barrier(core, pool=True):
    for e in core.engines:
        if e.n:
            e.wait((e.sem, e.n))
    meet = [e for e in core.nc.engines if pool or e != mybir.EngineType.Pool]
    core.nc.multi_engine_barrier(meet, sems_to_clear=core.ticks)
    for e in core.engines:
        e.n = 0
    core.ev.clear()


def loop(core, n):
    barrier(core)
    return core.nc.Fori(0, n)


def const(core, name):
    return core.cpack.view(core.consts, name)


def vec(core, name):
    return core.vpack.view(core.vecs.ap, name)


def begin(core):
    nc, t = core.nc, core.t
    names = ["PE", "ACT", "DVE", "POOL", "SP"]
    sems = [sem(core, "tick_" + n) for n in names]
    assert [s.num for s in sems] == list(range(sems[0].num, sems[0].num + 5))
    core.ticks = range(sems[0].num, sems[0].num + 5)
    engs = [nc.tensor, nc.scalar, nc.vector, nc.gpsimd, nc.sync]
    core.engines = [Engine(e, s) for e, s in zip(engs, sems)]
    core.pe, core.act, core.dve, core.pool, core.sp = core.engines
    core.x = sb(core, "x", [P, KT, T])
    core.u = sb(core, "u", [P, KT, T])
    core.small = sb(core, "small", [P, 512])
    core.rs = sb(core, "rs", [P, T])
    core.sq = [sb(core, f"square{b}", [P, T]) for b in range(2)]
    core.eps = sb(core, "eps", [P, 1])
    core.bank = [core.stack.enter_context(nc.psum_tensor(f"bank{b}", [P, T], F32)).ap() for b in range(8)]
    core.free = [None] * 8
    core.vecs = landing(core, "vecs", [P, core.vpack.width])
    core.cland = landing(core, "consts", [P, core.cpack.width])
    core.consts = core.cland.ap
    core.dense = core.stack.enter_context(ExitStack())
    core.ring = [landing(core, f"ring{s}", [P, KT, P], core.dense) for s in range(RING)]
    xl = Landing(core.x, sem(core, "landed_x"))
    xl.load(core.sp, t["xT"])
    core.cland.load(core.sp, t["consts"])
    core.vecs.load(core.sp, t["vecs"])
    for s in range(RING):
        core.ring[s].load(core.sp, chunk(core, s))
    for e in (core.pe, core.act, core.dve, core.pool):
        for l in (xl, core.cland, core.vecs):
            e.eng.wait_ge(l.sem, 16)
    core.dve.done(core.dve.eng.memset(core.eps, EPS))
    barrier(core)


def chunk(core, at):
    if isinstance(at, int):
        w = core.t["dense"][at:at + 1]
    else:
        w = core.t["dense"][bass.ds(at, 1)]
    return w.rearrange("o p (k m) -> p (o k) m", m=P)


def tile_products(core, slot, rhs, bank, start=True, stop=True, after=()):
    core.pe.wait(core.ev["bank read", bank] if start else None, *after)
    core.ring[slot].wait(core.pe)
    for k in range(KT):
        ins = core.pe.eng.matmul(core.bank[bank], core.ring[slot].ap[:, k, :], rhs(k),
                                 start=start and k == 0, stop=stop and k == KT - 1)
    return core.pe.done(ins)


def refill(core, slot, at, used):
    if at is None:
        return
    core.ring[slot].load(core.sp, chunk(core, at), used)


def evacuate(core, bank, dst, tick, n, after=()):
    e = (core.act, core.dve)[n % 2]
    e.wait(tick, *after)
    if n % 2:
        t = e.done(e.eng.tensor_copy(dst, core.bank[bank]))
    else:
        t = e.done(e.eng.copy(dst, core.bank[bank]))
    core.ev["bank read", bank] = t
    return t


def project(core, first, n, y):
    with loop(core, n // RING) as i:
        for j in range(RING):
            tick = tile_products(core, j, lambda k: core.u[:, k, :], j)
            refill(core, j, i * RING + (first + j + RING), tick)
            evacuate(core, j, y[:, bass.ds(i * RING + j, 1), :].rearrange("p o t -> p (o t)"), tick, j)
        barrier(core)


def add_projection(core, first, ready=()):
    for j in range(N_O):
        tick = tile_products(core, j, lambda k: core.u[:, k, :], j, after=ready)
        nxt = first + j + RING
        refill(core, j, nxt if nxt < N_CH else None, tick)
        core.dve.wait(tick)
        core.ev["bank read", j] = core.dve.done(core.dve.eng.tensor_tensor(
            core.x[:, j, :], core.x[:, j, :], core.bank[j], ALU.add))
    barrier(core)


def sum_squares(core, tiles, weights, bank, after=()):
    for k, src in enumerate(tiles):
        sq = core.sq[k % 2]
        core.act.wait(core.ev["square summed", k % 2], *after)
        t = core.act.done(core.act.eng.activation(sq, src, ACT.Square))
        core.pe.wait(t, core.ev["bank read", bank] if k == 0 else None)
        core.ev["square summed", k % 2] = core.pe.done(core.pe.eng.matmul(
            core.bank[bank], weights, sq, start=k == 0, stop=k == len(tiles) - 1))
    return core.ev["square summed", (len(tiles) - 1) % 2]


def inverse_root(core, dst, src, n, width_tick):
    core.act.wait(width_tick)
    t = core.act.done(core.act.eng.activation(dst, src, ACT.Ln, bias=core.eps[0:dst.shape[0]], scale=1.0 / n))
    core.act.wait(t)
    return t, core.act.done(core.act.eng.activation(dst, dst, ACT.Exp, scale=-0.5))


def norm(core, gain, dst):
    tick = sum_squares(core, [core.x[:, k, :] for k in range(KT)], const(core, "ones"), 7)
    core.ev["bank read", 7], t = inverse_root(core, core.rs, core.bank[7], D, tick)
    core.dve.wait(t)
    for k in range(KT):
        t = core.dve.done(core.dve.eng.scalar_tensor_tensor(
            dst[:, k, :], core.x[:, k, :], vec(core, gain)[:, k:k + 1], core.rs, ALU.mult, ALU.mult))
    barrier(core)


def mlp(core, first, gain):
    norm(core, gain, core.u)
    with ExitStack() as st:
        h = sb(core, "h", [P, FT, T], stack=st)
        r = [sb(core, f"relu{b}", [P, T], stack=st) for b in range(2)]
        with loop(core, FT // RING) as i:
            used = [None, None]
            for j in range(RING):
                tick = tile_products(core, j, lambda k: core.u[:, k, :], j)
                refill(core, j, i * RING + (first + j + RING), tick)
                core.act.wait(tick, used[j % 2])
                t = core.act.done(core.act.eng.activation(r[j % 2], core.bank[j], ACT.Relu))
                core.ev["bank read", j] = t
                core.dve.wait(t)
                used[j % 2] = core.dve.done(core.dve.eng.tensor_tensor(
                    h[:, bass.ds(i * RING + j, 1), :].rearrange("p o t -> p (o t)"),
                    r[j % 2], r[j % 2], ALU.mult))
            barrier(core)
        per = FT // KT
        with loop(core, FT // RING) as i:
            for m in range(RING // per):
                for q in range(per):
                    s = m * per + q
                    tick = tile_products(core, s, lambda k: h[:, q * KT + k, :], m, start=q == 0, stop=q == per - 1)
                    refill(core, s, i * RING + (first + FT + s + RING), tick)
                core.dve.wait(tick)
                xm = core.x[:, bass.ds(i * (RING // per) + m, 1), :].rearrange("p o t -> p (o t)")
                core.ev["bank read", m] = core.dve.done(core.dve.eng.tensor_tensor(xm, xm, core.bank[m], ALU.add))
            barrier(core)


def rope(core, dst, src, c, s, bank, tmp, ready=()):
    core.pe.wait(core.ev["bank read", bank], *ready)
    t = core.pe.done(core.pe.eng.matmul(core.bank[bank], const(core, "swap"), src, start=True, stop=True))
    core.dve.wait(*ready)
    core.dve.done(core.dve.eng.tensor_tensor(tmp[:, 0:T], src, const(core, c), ALU.mult))
    core.dve.wait(t)
    t = core.ev["bank read", bank] = core.dve.done(core.dve.eng.tensor_tensor(tmp[:, T:], core.bank[bank], const(core, s), ALU.mult))
    core.dve.wait(t)
    return core.dve.done(core.dve.eng.tensor_tensor(dst, tmp[:, 0:T], tmp[:, T:], ALU.add))


def to_tokens(core, dst, tiles, after=()):
    for b in range(NB):
        bank = b % 4
        core.pe.wait(core.ev["bank read", bank], *after)
        for m, src in enumerate(tiles):
            ins = core.pe.eng.transpose(core.bank[bank][:, m * P:(m + 1) * P], src[:, b * P:(b + 1) * P], const(core, "ident"))
        t = core.pe.done(ins)
        e = (core.act, core.dve)[b % 2]
        e.wait(t)
        copy = e.eng.tensor_copy if b % 2 else e.eng.copy
        w = len(tiles) * P
        t = core.ev["bank read", bank] = e.done(copy(dst[:, b, 0:w], core.bank[bank][:, 0:w]))
    return t


def staged(core, units):
    depth = max(len(u) for u in units)
    for step in range(len(units) + depth - 1):
        for s in reversed(range(depth)):
            n = step - s
            if 0 <= n < len(units) and s < len(units[n]):
                units[n][s]()


def soft_buffers(core, st):
    core.E = [sb(core, f"exp{b}", [P, T], stack=st) for b in range(3)]
    core.ET = [sb(core, f"expT{b}", [P, T], stack=st) for b in range(2)]
    core.qs = sb(core, "q_pair", [P, T], stack=st)
    core.ks = sb(core, "k_pair", [P, T], stack=st)
    core.ro = sb(core, "rope_tmp", [P, 2 * T], stack=st)
    core.on = sb(core, "o_tokens", [P, NB, P], stack=st)


def softmax(core, n, b, logits, mask, ready):
    e, lb = core.E[n % 3], n % 3
    note = {}
    neg, total = core.small[:, 2 * n:2 * n + 1], core.small[:, 2 * n + 1:2 * n + 2]

    def first():
        core.pe.wait(core.ev["bank read", lb], *ready)
        w = P * (b + 1)
        note["logits"] = core.pe.done(logits(core.bank[lb][:, 0:w], b))

    def second():
        w = P * (b + 1)
        core.dve.wait(note["logits"], core.ev["exp turned", n % 3])
        t = core.ev["bank read", lb] = core.dve.done(core.dve.eng.tensor_tensor_reduce(
            e[:, 0:w], core.bank[lb][:, 0:w], mask(b), -1.0, 3.0e38, ALU.add, ALU.min, neg))
        core.act.wait(t)
        note["exp"] = core.act.done(core.act.eng.activation(
            e[:, 0:w], e[:, 0:w], ACT.Exp, bias=neg, scale=-1.0, accum_out=total))
    note["e"], note["total"] = e, total
    return [first, second], note


def times_values(core, n, b, note, key, values, width, out, finish):
    tb, ob = 3 + n % 2, 5 + n % 2
    eT = core.ET[n % 2]

    def third():
        w = P * (b + 1)
        core.pe.wait(note[key], core.ev["bank read", tb])
        for j in range(b + 1):
            ins = core.pe.eng.transpose(core.bank[tb][:, j * P:(j + 1) * P], note["e"][:, j * P:(j + 1) * P], const(core, "ident"))
        t = core.pe.done(ins)
        core.ev["exp turned", note.get("slot", n % 3)] = t
        en = (core.act, core.dve)[n % 2]
        en.wait(t, core.ev["expT used", n % 2])
        copy = en.eng.tensor_copy if n % 2 else en.eng.copy
        note["eT"] = core.ev["bank read", tb] = en.done(copy(eT[:, 0:w], core.bank[tb][:, 0:w]))

    def fourth():
        core.pe.wait(note["eT"], core.ev["bank read", ob])
        for j in range(b + 1):
            ins = core.pe.eng.matmul(core.bank[ob][:, 0:width], eT[:, j * P:(j + 1) * P], values(j),
                                     start=j == 0, stop=j == b)
        t = core.ev["expT used", n % 2] = core.pe.done(ins)
        finish(core.bank[ob][:, 0:width], t, ob)
    return [third, fourth]


def normalised(core, n, dst, note):
    inv = core.small[:, 128 + n:129 + n]

    def finish(product, tick, ob):
        core.dve.wait(note["exp"])
        t = core.dve.done(core.dve.eng.reciprocal(inv, note["total"]))
        core.dve.wait(t, tick)
        core.ev["heads written"] = core.ev["bank read", ob] = core.dve.done(core.dve.eng.tensor_scalar(dst, product, inv, None, ALU.mult))
    return finish


def store_heads(core, m, ready, bank=7):
    core.pe.wait(core.ev["bank read", bank], *ready)
    for b in range(NB):
        ins = core.pe.eng.transpose(core.bank[bank][:, b * P:(b + 1) * P], core.on[:, b, :], const(core, "ident"))
    t = core.pe.done(ins)
    core.act.wait(t)
    core.ev["bank read", bank] = core.act.done(core.act.eng.copy(
        core.u[:, bass.ds(m, 1), :].rearrange("p o t -> p (o t)"), core.bank[bank]))


def causal(core, b):
    return const(core, "causal")[:, T - P * (b + 1):T]


def pair_products(core, a, q=None, k=None):
    q, k = q if q is not None else core.qs, k if k is not None else core.ks
    r = slice(a * HD, (a + 1) * HD)

    def logits(out, b):
        return core.pe.eng.matmul(out, q[r, b * P:(b + 1) * P], k[r, 0:P * (b + 1)], start=True, stop=True)
    return logits


def layer_ab(core):
    nc, pe, act, dve = core.nc, core.pe, core.act, core.dve
    norm(core, "g_a0", core.u)
    with ExitStack() as st:
        y = sb(core, "y_ab", [P, N_AB, T], stack=st)
        AQ, AQI, BQ, BK, CKV, MI, MF, BV = 0, 4, 8, 12, 16, 18, 19, 20
        with ExitStack() as stw:
            project(core, CH_AB, N_AB, y)
        soft_buffers(core, st)
        wuk = landing(core, "w_uk", [P, 2, T], st)
        wuv = landing(core, "w_uv", [P, 2, T], st)
        wuk.load(core.sp, core.t["w_uk"])
        wuv.load(core.sp, core.t["w_uv"])
        vb = sb(core, "v_fox", [P, NB, T], stack=st)
        vd = sb(core, "v_dsa", [P, NB, T], stack=st)
        kd = sb(core, "k_dsa", [P, NB, T], stack=st)
        add = sb(core, "dsa_mask", [P, 3, T], stack=st)
        ki = y[:, BV, :]
        tok = core.on
        to_tokens(core, vb, [y[:, BV + m, :] for m in range(4)])
        tok_t = to_tokens(core, tok, [y[:, MF, :]])
        ck = [y[:, CKV + r, :] for r in range(2)]
        t = sum_squares(core, ck, const(core, "ones"), 7)
        core.ev["bank read", 7], t = inverse_root(core, core.rs, core.bank[7], 256, t)
        dve.wait(t)
        for r in range(2):
            ckt = dve.done(dve.eng.scalar_tensor_tensor(ck[r], ck[r], vec(core, "g_kv")[:, r:r + 1], core.rs, ALU.mult, ALU.mult))
        mi = y[:, MI, :]
        act.wait(ckt)
        t = sum_squares(core, [mi], const(core, "pair_ones"), 6, after=(ckt,))
        core.ev["bank read", 6], t = inverse_root(core, core.rs[0:HD], core.bank[6][0:HD], HD, t)
        dve.wait(t)
        t = dve.done(dve.eng.scalar_tensor_tensor(mi[0:HD], mi[0:HD], vec(core, "g_ki")[0:HD], core.rs[0:HD], ALU.mult, ALU.mult))
        dve.wait(t)
        t = rope(core, mi, mi, "rope_c", "rope_s", 5, core.ro, (t,))
        pe.wait(t, core.ev["bank read", 4])
        t = pe.done(pe.eng.matmul(core.bank[4], const(core, "dup"), mi, start=True, stop=True))
        act.wait(t)
        core.ev["bank read", 4] = act.done(act.eng.copy(ki, core.bank[4]))
        wuk.wait(pe)
        wuv.wait(pe)
        pe.wait(ckt)
        for m in range(4):
            pe.wait(core.ev["bank read", m])
            for r in range(2):
                pe.eng.matmul(core.bank[m], wuk.ap[:, r, m * P:(m + 1) * P], ck[r], start=r == 0, stop=False)
            t = pe.done(pe.eng.matmul(core.bank[m], const(core, "sel_rope"), mi, start=False, stop=True))
            evacuate(core, m, kd[:, m, :], t, m)
        for b in range(NB):
            pe.wait(core.ev["bank read", b])
            for r in range(2):
                ins = pe.eng.matmul(core.bank[b], ck[r][:, b * P:(b + 1) * P], wuv.ap[:, r, :], start=r == 0, stop=r == 1)
            evacuate(core, b, vd[:, b, :], pe.done(ins), b)
        dve.wait(tok_t)
        wsc = sb(core, "w_idx", [P, NB, 8], stack=st)
        dve.done(dve.eng.tensor_scalar(wsc, tok[:, :, 32:40], 8 ** -0.5 * HD ** -0.5, None, ALU.mult))
        dve.done(dve.eng.memset(add, 0.0))
        with loop(core, 4) as m:
            qt = rope(core, core.qs, y[:, bass.ds(m + AQI, 1), :].rearrange("p o t -> p (o t)"), "rope_c", "rope_s", 7, core.ro)
            n = 0
            rel_free = [None] * 3
            for b in (1, 2, 3):
                w = P * (b + 1)
                for a in range(2):
                    pe.wait(qt, core.ev["bank read", n % 3])
                    t = pe.done(pair_products(core, a, k=ki)(core.bank[n % 3][:, 0:w], b))
                    act.wait(t, rel_free[n % 3])
                    t = core.ev["bank read", n % 3] = act.done(act.eng.activation(core.E[n % 3][:, 0:w], core.bank[n % 3][:, 0:w], ACT.Relu))
                    dve.wait(t)
                    t = rel_free[n % 3] = dve.done(dve.eng.scalar_tensor_tensor(
                        add[:, b - 1, 0:w], core.E[n % 3][:, 0:w], wsc[:, b, bass.ds(m * 2 + a, 1)],
                        add[:, b - 1, 0:w], ALU.mult, ALU.add))
                    dve.wait(t)
                    n += 1
            barrier(core)
        cum, fl, fr = y[:, BV:BV + 4, :], y[:, AQI, :], y[:, AQI + 1, :]
        z, a, s = core.E[0][0:8], core.E[1][0:8], core.E[2][0:8]
        t = dve.done(dve.eng.tensor_scalar(z, y[0:8, MF, :], vec(core, "b_f")[0:8], None, ALU.add))
        dve.wait(t)
        t = dve.done(dve.eng.scalar_tensor_tensor(a, z, -1.0, z, ALU.mult, ALU.min))
        act.wait(t)
        t = act.done(act.eng.activation(a, a, ACT.Exp))
        act.wait(t)
        t = act.done(act.eng.activation(a, a, ACT.Ln, bias=1.0))
        dve.wait(t)
        t = dve.done(dve.eng.scalar_tensor_tensor(a, z, 0.0, a, ALU.min, ALU.subtract))
        dve.wait(t)
        t = dve.done(dve.eng.tensor_tensor_scan(s, const(core, "ones")[0:8, 0:1].to_broadcast([8, T]), a, 0.0, ALU.mult, ALU.add))
        dve.wait(t)
        t = dve.done(dve.eng.tensor_scalar(a, s, -1.0, None, ALU.mult))
        cum_l = Landing(None, sem(core, "landed_cum"))
        core.sp.wait(t)
        for h in range(8):
            for r, src in ((0, a), (32, s)):
                row = HD * (h % 2) + r
                core.sp.eng.dma_start(cum[row:row + 1, h // 2, :], src[h:h + 1]).then_inc(cum_l.sem, 16)
        dve.eng.wait_ge(cum_l.sem, 16 * 16)
        t = dve.done(dve.eng.memset(fl, 0.0))
        t = dve.done(dve.eng.memset(fr, 0.0))
        dve.wait(t)
        for a in range(2):
            dve.done(dve.eng.memset(fl[HD * a:HD * a + 1], 1.0))
            dve.done(dve.eng.memset(fr[HD * a + 32:HD * a + 33], 1.0))
        top = core.small[:, 0:24]
        for b in (1, 2, 3):
            s = add[:, b - 1, 0:P * (b + 1)]
            t = dve.done(dve.eng.tensor_tensor(s, s, causal(core, b), ALU.add))
        dve.wait(t)
        for r in range(TOPK // 8):
            for b in (1, 2, 3):
                t = dve.done(dve.eng.max(top[:, 8 * (b - 1):8 * b], add[:, b - 1, 0:P * (b + 1)]))
            dve.wait(t)
            for b in (1, 2, 3):
                s = add[:, b - 1, 0:P * (b + 1)]
                t = dve.done(dve.eng.match_replace(s, top[:, 8 * (b - 1):8 * b], s, TAKEN))
            dve.wait(t)
        for b in (1, 2, 3):
            s = add[:, b - 1, 0:P * (b + 1)]
            dve.done(dve.eng.tensor_scalar(s, s, TAKEN / 2, NEG, ALU.is_gt, ALU.mult))
        with loop(core, 4) as m:
            dve.done(dve.eng.tensor_copy(core.ks, kd[:, bass.ds(m, 1), :].rearrange("p o t -> p (o t)")))
            qt = rope(core, core.qs, y[:, bass.ds(m + AQ, 1), :].rearrange("p o t -> p (o t)"), "rope_cq", "rope_sq", 7, core.ro)
            mask = lambda b: causal(core, 0) if b == 0 else add[:, b - 1, 0:P * (b + 1)]
            pair_attention(core, m, qt, lambda a: pair_products(core, a), mask, vd)
            barrier(core)
        with loop(core, 4) as m:
            t = dve.done(dve.eng.tensor_copy(core.ks, y[:, bass.ds(m + BK, 1), :].rearrange("p o t -> p (o t)")))
            t = dve.done(dve.eng.tensor_scalar(core.qs, y[:, bass.ds(m + BQ, 1), :].rearrange("p o t -> p (o t)"), SCALE, None, ALU.mult))
            for a in range(2):
                for row, dst in ((HD * a, fr), (HD * a + 32, fl)):
                    qt = dve.done(dve.eng.tensor_copy(
                        dst[row:row + 1], cum[row:row + 1, bass.ds(m, 1), :].rearrange("p o t -> p (o t)")))

            def products(a):
                main = pair_products(core, a)

                def logits(out, b):
                    r = slice(a * HD, (a + 1) * HD)
                    pe.eng.matmul(out, core.qs[r, b * P:(b + 1) * P], core.ks[r, 0:P * (b + 1)], start=True, stop=False)
                    return pe.eng.matmul(out, fl[r, b * P:(b + 1) * P], fr[r, 0:P * (b + 1)], start=False, stop=True)
                return logits
            pair_attention(core, m, qt, products, lambda b: causal(core, b), vb, out=m + 4)
            barrier(core)
    add_projection(core, CH_ABO)


def pair_attention(core, m, qt, products, mask, values, out=None):
    units, n = [], 0
    for b in range(NB):
        for a in range(2):
            s, note = softmax(core, n, b, products(a), mask, (qt,))
            dst = core.on[:, b, a * HD:(a + 1) * HD]
            val = lambda j, a=a: values[:, j, bass.ds(m * P + a * HD, HD)]
            units.append(s + times_values(core, n, b, note, "exp", val, HD, None, normalised(core, n, dst, note)))
            n += 1
    staged(core, units)
    store_heads(core, m if out is None else out, (core.ev["heads written"],))




def layer_c(core):
    pe, act, dve = core.pe, core.act, core.dve
    norm(core, "g_a1", core.u)
    with ExitStack() as st:
        y = sb(core, "y_c", [P, N_C, T], stack=st)
        KC, KS, KW, VC, VS, VW, GL = 8, 9, 10, 11, 12, 13, 14
        project(core, CH_C, N_C, y)
        soft_buffers(core, st)
        w1 = {n: landing(core, f"cmp_{n}1", [P, CMP_LEN, P], st) for n in "kv"}
        k2 = landing(core, "cmp_k2", [P, 2, P], st)
        v2 = landing(core, "cmp_v2", [P, HD], st)
        for n in "kv":
            w1[n].load(core.sp, core.t[f"cmp_{n}1"])
        k2.load(core.sp, core.t["cmp_k2"])
        v2.load(core.sp, core.t["cmp_v2"])
        vs = sb(core, "v_sel", [P, NB, P], stack=st)
        vw = sb(core, "v_win", [P, NB, P], stack=st)
        gt = sb(core, "gates", [P, NB, P], stack=st)
        to_tokens(core, vs, [y[:, VS, :]])
        to_tokens(core, vw, [y[:, VW, :]])
        t = to_tokens(core, gt, [y[:, GL, :]])
        g = gt[:, :, 0:48]
        dve.wait(t)
        dve.wait(core.ev["bank read", 0], core.ev["bank read", 1], core.ev["bank read", 2], core.ev["bank read", 3])
        t = dve.done(dve.eng.tensor_tensor(g, g, vec(core, "b_gate").unsqueeze(1).to_broadcast([P, NB, 48]), ALU.add))
        act.wait(t)
        t = act.done(act.eng.activation(g, g, ACT.Exp, scale=-1.0))
        dve.wait(t)
        t = dve.done(dve.eng.tensor_scalar(g, g, 1.0, None, ALU.add))
        dve.wait(t)
        dve.done(dve.eng.reciprocal(g, g))
        t = None
        for j in (KC, KS, KW):
            t = rope(core, y[:, j, :], y[:, j, :], "rope_c", "rope_s", 4 + j % 2, core.ro, (t,))
            dve.wait(t)
        xg = {n: sb(core, f"win_{n}", [P, CMP_LEN, 32], stack=st) for n in "kv"}
        ready = {}
        for n, j in (("k", KC), ("v", VC)):
            wins = y[:, j, :].rearrange("p (n l) -> p l n", l=CMP_STRIDE)
            dve.done(dve.eng.tensor_copy(xg[n][:, 0:16, 0:N_CMP], wins[:, :, 0:N_CMP]))
            dve.done(dve.eng.tensor_copy(xg[n][:, 16:32, 0:N_CMP], wins[:, :, 1:N_CMP + 1]))
            ready[n] = dve.done(dve.eng.tensor_copy(xg[n][:, :, N_CMP:32], vec(core, "pe_" + n).unsqueeze(2)))
        hid = sb(core, "hid", [P, 4, 32], stack=st)
        hz = sb(core, "hid_z", [P, 4, 32], stack=st)
        for x, n in enumerate("kv"):
            w1[n].wait(pe)
            for a in range(2):
                r = slice(a * HD, (a + 1) * HD)
                q = 2 * x + a
                pe.wait(ready[n], core.ev["bank read", q])
                for l in range(CMP_LEN):
                    ins = pe.eng.matmul(core.bank[q][:, 0:32], w1[n].ap[r, l, :], xg[n][r, l, :],
                                        start=l == 0, stop=l == CMP_LEN - 1)
                t = pe.done(ins)
                dve.wait(t)
                t = core.ev["bank read", q] = dve.done(dve.eng.tensor_copy(hid[:, q, :], core.bank[q][:, 0:32]))
        dve.wait(t)
        seq = []
        two_c = 2.0 * float(np.sqrt(2.0 / np.pi))
        t = dve.done(dve.eng.tensor_tensor(hid[:, :, 0:N_CMP], hid[:, :, 0:N_CMP],
                                           hid[:, :, N_CMP:32].to_broadcast([P, 4, N_CMP]), ALU.add))
        dve.wait(t)
        t = dve.done(dve.eng.tensor_tensor(hz, hid, hid, ALU.mult))
        dve.wait(t)
        t = dve.done(dve.eng.tensor_scalar(hz, hz, 0.044715, 1.0, ALU.mult, ALU.add))
        dve.wait(t)
        t = dve.done(dve.eng.tensor_tensor(hz, hz, hid, ALU.mult))
        act.wait(t)
        t = act.done(act.eng.activation(hz, hz, ACT.Exp, scale=-two_c))
        dve.wait(t)
        t = dve.done(dve.eng.tensor_scalar(hz, hz, 1.0, None, ALU.add))
        dve.wait(t)
        t = dve.done(dve.eng.reciprocal(hz, hz))
        dve.wait(t)
        t = dve.done(dve.eng.tensor_tensor(hid, hid, hz, ALU.mult))
        dve.wait(t)
        kc = sb(core, "k_cmp", [P, 32], stack=st)
        rep = sb(core, "hid_rep", [P, 4, 32], stack=st)
        vcd = sb(core, "v_cmp", [P, 4, HD], stack=st)
        dve.done(dve.eng.tensor_copy(rep[:, 0:2], hid[:, 2:4]))
        tr = dve.done(dve.eng.tensor_copy(rep[:, 2:4], hid[:, 2:4]))
        t2 = dve.done(dve.eng.memset(vcd, 0.0))
        k2.wait(pe)
        v2.wait(pe)
        pe.wait(t, tr, core.ev["bank read", 0], core.ev["bank read", 1])
        for a in range(2):
            ins = pe.eng.matmul(core.bank[0][:, 0:32], k2.ap[:, a, :], hid[:, a, :], start=a == 0, stop=a == 1)
        t = pe.done(ins)
        dve.wait(t)
        core.ev["bank read", 0] = dve.done(dve.eng.tensor_copy(kc, core.bank[0][:, 0:32]))
        t = pe.done(pe.eng.matmul(core.bank[1][:, 0:HD], rep.rearrange("p a n -> p (a n)"), v2.ap, start=True, stop=True))
        dve.wait(t, t2)
        for r in range(4):
            t = dve.done(dve.eng.tensor_copy(vcd[32 * r:32 * r + 32, r, :], core.bank[1][32 * r:32 * r + 32, 0:HD]))
        core.ev["bank read", 1] = t
        pc = sb(core, "p_cmp", [P, 8, 32], stack=st)
        pcT = sb(core, "p_cmpT", [P, 2, P], stack=st)
        gs = sb(core, "gate_pair", [P, NB, 6], stack=st)
        vsp = sb(core, "v_pair", [P, 2, NB, P], stack=st)
        dve.wait(t)
        with loop(core, 8) as m:
            tg = dve.done(dve.eng.tensor_copy(gs, gt[:, :, bass.ds(m * 6, 6)]))
            qt = rope(core, core.qs, y[:, bass.ds(m, 1), :].rearrange("p o t -> p (o t)"), "rope_cq", "rope_sq", 7, core.ro)
            pe.wait(qt, core.ev["bank read", 3], core.ev["bank read", 4])
            for a in range(2):
                r = slice(a * HD, (a + 1) * HD)
                for b in range(NB):
                    ins = pe.eng.matmul(core.bank[3 + a][:, b * 32:(b + 1) * 32],
                                        core.qs[r, b * P:(b + 1) * P], kc[r, :], start=True, stop=True)
            t = pe.done(ins)
            mx, sm = core.small[:, 300:308], core.small[:, 310:318]
            flat = pc.rearrange("p a n -> p (a n)")
            bc = lambda v: v.unsqueeze(2).to_broadcast([P, 8, 32])
            dve.wait(t)
            for a in range(2):
                t = core.ev["bank read", 3 + a] = dve.done(dve.eng.tensor_tensor(
                    pc[:, a::2, :], core.bank[3 + a][:, 0:P].rearrange("p (b n) -> p b n", n=32),
                    const(core, "cmp_add").rearrange("p (b a n) -> p b a n", a=2, n=32)[:, :, a, :], ALU.add))
            dve.wait(t)
            t = dve.done(dve.eng.tensor_reduce(mx, pc, AX.X, ALU.max))
            dve.wait(t)
            t = dve.done(dve.eng.tensor_tensor(pc, pc, bc(mx), ALU.subtract))
            act.wait(t)
            t = act.done(act.eng.activation(pc, pc, ACT.Exp))
            dve.wait(t)
            t = dve.done(dve.eng.tensor_tensor(flat, flat, const(core, "cmp_one"), ALU.mult))
            dve.wait(t)
            t = dve.done(dve.eng.tensor_reduce(sm, pc, AX.X, ALU.add))
            dve.wait(t)
            t = dve.done(dve.eng.tensor_scalar(sm, sm, 1e-30, None, ALU.max))
            dve.wait(t)
            t = dve.done(dve.eng.reciprocal(sm, sm))
            dve.wait(t, tg)
            t = dve.done(dve.eng.tensor_tensor(sm.rearrange("p (b a) -> p b a", a=2), sm.rearrange("p (b a) -> p b a", a=2),
                                               gs[:, :, 0:4:3], ALU.mult))
            dve.wait(t)
            t = dve.done(dve.eng.tensor_tensor(pc, pc, bc(sm), ALU.mult))
            pe.wait(t, core.ev["bank read", 4])
            for h in range(2):
                ins = pe.eng.transpose(core.bank[4][:, h * P:(h + 1) * P], flat[:, h * P:(h + 1) * P], const(core, "ident"))
            t = pe.done(ins)
            act.wait(t)
            t = core.ev["bank read", 4] = act.done(act.eng.copy(pcT.rearrange("p h q -> p (h q)"), core.bank[4][:, 0:256]))
            pe.wait(t, core.ev["bank read", 5])
            for h in range(2):
                ins = pe.eng.matmul(core.bank[5][:, h * 256:(h + 1) * 256], pcT[:, h, :], vcd.rearrange("p r d -> p (r d)"),
                                    start=True, stop=True)
            t = pe.done(ins)
            act.wait(t)
            oc = core.ev["bank read", 5] = act.done(act.eng.copy(core.on.rearrange("p b d -> p (b d)"), core.bank[5]))
            units, n = [], 0
            for b in range(NB):
                for x, (kk, vv) in enumerate(((KS, vs), (KW, vw))):
                    for a in range(2):
                        s, note = softmax(core, n, b, pair_products(core, a, k=y[:, kk, :]), lambda b: causal(core, b), (qt,))
                        dst = core.on[:, b, a * HD:(a + 1) * HD]
                        val = lambda j, a=a, vv=vv: vv[:, j, a * HD:(a + 1) * HD]
                        fin = gated(core, n, dst, note, gs[:, b, 3 * a + 1 + x:3 * a + 2 + x], (b, a), (oc, tg))
                        units.append(s + times_values(core, n, b, note, "exp", val, HD, None, fin))
                        n += 1
            staged(core, units)
            store_heads(core, m, (core.ev["heads written"],))
            barrier(core)
    add_projection(core, CH_CO)


def gated(core, n, dst, note, gate, key, after):
    inv = core.small[:, 128 + n:129 + n]

    def finish(product, tick, ob):
        core.dve.wait(note["exp"])
        t = core.dve.done(core.dve.eng.reciprocal(inv, note["total"]))
        core.dve.wait(t, *after)
        t = core.dve.done(core.dve.eng.tensor_tensor(inv, inv, gate, ALU.mult))
        core.dve.wait(t, tick, core.ev["gated", key])
        core.ev["heads written"] = core.ev["bank read", ob] = core.ev["gated", key] = core.dve.done(
            core.dve.eng.scalar_tensor_tensor(dst, product, inv, dst, ALU.mult, ALU.add))
    return finish


def layer_2(core):
    pe, act, dve = core.pe, core.act, core.dve
    norm(core, "g_a2", core.u)
    with ExitStack() as st:
        y = sb(core, "y_2", [P, N_2, T], stack=st)
        DQ, DK, DV, SQ, SK, SV = 0, 4, 8, 12, 16, 20
        project(core, CH_2, N_2, y)
        soft_buffers(core, st)
        vd = sb(core, "v_da", [P, NB, T], stack=st)
        vb = sb(core, "v_sb", [P, NB, T], stack=st)
        to_tokens(core, vd, [y[:, DV + m, :] for m in range(4)])
        to_tokens(core, vb, [y[:, SV + m, :] for m in range(4)])
        bf = landing(core, "bias", [P, 4, T], st)
        row = sb(core, "bias_row", [P, LV], stack=st)
        scr_sem = sem(core, "bias_out")
        scr = core.nc.dram_tensor("bias_scratch", [4, P * LV], F32, kind="Internal").ap()
        for h in range(4):
            for q in range(2):
                w = T if q == 0 else LV - T
                pe.wait(core.ev["bank read", 4 + q])
                t = pe.done(pe.eng.matmul(core.bank[4 + q][:, 0:w], vec(core, "rel")[0:BUCKETS, h * P:(h + 1) * P],
                                          const(core, "buckets")[0:BUCKETS, q * T:q * T + w], start=True, stop=True))
                act.wait(t)
                if h and q == 0:
                    act.eng.wait_ge(scr_sem, 16 * h)
                t = core.ev["bank read", 4 + q] = act.done(act.eng.copy(row[:, q * T:q * T + w], core.bank[4 + q][:, 0:w]))
            core.sp.wait(t)
            core.sp.eng.dma_start(scr[h].rearrange("(p c) -> p c", c=LV), row).then_inc(scr_sem, 16)
        core.sp.eng.wait_ge(scr_sem, 64)
        for h in range(4):
            src = scr[h, P - 1:P - 1 + P * (LV - 1)].rearrange("(p c) -> p c", c=LV - 1)[:, 0:T]
            core.sp.eng.dma_start(bf.ap[:, h, :], src).then_inc(bf.sem, 16)
        lam = core.small[:, 400:404]
        lt = core.E[0][:, 0:P]
        lv = vec(core, "lam").rearrange("p (s x) -> p s x", s=2)
        t = dve.done(dve.eng.tensor_tensor(lt, lv[:, 0, :], lv[:, 1, :], ALU.mult))
        dve.wait(t)
        t = dve.done(dve.eng.tensor_reduce(lam[:, 0:2], lt.rearrange("p (s x) -> p s x", s=2), AX.X, ALU.add))
        act.wait(t)
        t = act.done(act.eng.activation(lam[:, 0:2], lam[:, 0:2], ACT.Exp))
        dve.wait(t)
        t = dve.done(dve.eng.tensor_tensor(lam[:, 2:3], lam[:, 0:1], lam[:, 1:2], ALU.subtract))
        dve.wait(t)
        t = dve.done(dve.eng.tensor_scalar(lam[:, 3:4], lam[:, 2:3], LAMBDA_INIT, None, ALU.add))
        sg = sb(core, "subln_s", [P, P], stack=st)
        gq = sb(core, "gq_s", [P, 1], stack=st)
        dve.done(dve.eng.tensor_scalar(sg, vec(core, "subln"), 1.0 - LAMBDA_INIT, None, ALU.mult))
        dve.done(dve.eng.tensor_scalar(gq, vec(core, "g_qn"), SCALE, None, ALU.mult))
        dve.eng.wait_ge(bf.sem, 64)
        t = dve.done(dve.eng.tensor_tensor(bf.ap, bf.ap, const(core, "chunked").unsqueeze(1).to_broadcast([P, 4, T]), ALU.add))
        bm = sb(core, "bias_head", [P, T], stack=st)
        sq = sb(core, "sq_tok", [P, NB, P], stack=st)
        ssq = [sb(core, f"sq_head{q}", [P, T], stack=st) for q in range(2)]
        rsq = [sb(core, f"rs_head{q}", [P, T], stack=st) for q in range(2)]
        with loop(core, 4) as m:
            tb = dve.done(dve.eng.tensor_copy(bm, bf.ap[:, bass.ds(m, 1), :].rearrange("p o t -> p (o t)")))
            for q, (src, gain, dst) in enumerate(((DQ, gq, core.qs), (DK, vec(core, "g_kn"), core.ks))):
                s = y[:, bass.ds(m + src, 1), :].rearrange("p o t -> p (o t)")
                t = act.done(act.eng.activation(ssq[q], s, ACT.Square))
                pe.wait(t, core.ev["bank read", 6 + q])
                t = pe.done(pe.eng.matmul(core.bank[6 + q], const(core, "pair_ones"), ssq[q], start=True, stop=True))
                core.ev["bank read", 6 + q], t = inverse_root(core, rsq[q], core.bank[6 + q], HD, t)
                dve.wait(t)
                qt = dve.done(dve.eng.scalar_tensor_tensor(dst, s, gain[:, 0:1], rsq[q], ALU.mult, ALU.mult))
            units = []
            for b in range(NB):
                n0, n1 = 2 * b, 2 * b + 1
                mask = lambda b: bm[:, T - P * (b + 1):T]
                s0, note0 = softmax(core, n0, b, pair_products(core, 0), mask, (qt,))
                s1, note1 = softmax(core, n1, b, pair_products(core, 1), mask, (qt,))
                units.append(s0)
                units.append(s1 + [difference(core, b, n0, n1, note0, note1, lam)]
                             + times_values(core, n0 // 2 + 0, b, note0, "diff",
                                                 lambda j: vd[:, j, bass.ds(m * P, P)], P, None, plain(core, b)))
            staged(core, units)
            head_norm(core, sq, core.on, NB, P, sg.unsqueeze(1).to_broadcast([P, NB, P]))
            store_heads(core, m, (core.ev["heads written"],))
            barrier(core)
        zs = [y[:, DQ + j, :] for j in range(4)]
        sp_ = [y[:, DK + j, :] for j in range(4)]
        with loop(core, 4) as m:
            dve.done(dve.eng.tensor_copy(core.ks, y[:, bass.ds(m + SK, 1), :].rearrange("p o t -> p (o t)")))
            qt = dve.done(dve.eng.tensor_scalar(core.qs, y[:, bass.ds(m + SQ, 1), :].rearrange("p o t -> p (o t)"), SCALE, None, ALU.mult))
            z_free = [None] * 4
            s_free = [None] * 4
            for a in range(2):
                r = slice(a * HD, (a + 1) * HD)
                spt, zt, at = {}, {}, {}
                for j in range(3, -1, -1):
                    w = T - P * j
                    z, e, s = zs[j][:, 0:w], core.E[j % 2][:, 0:w], sp_[j][:, 0:w]
                    pe.wait(qt, core.ev["bank read", j])
                    t = pe.done(pe.eng.matmul(core.bank[j][:, 0:w], core.ks[r, j * P:(j + 1) * P], core.qs[r, j * P:T], start=True, stop=True))
                    dve.wait(t, z_free[j])
                    t = dve.done(dve.eng.tensor_tensor(z[:, 0:P], core.bank[j][:, 0:P], const(core, "strict"), ALU.add))
                    if w > P:
                        t = dve.done(dve.eng.tensor_copy(z[:, P:w], core.bank[j][:, P:w]))
                    core.ev["bank read", j] = zt[j] = t
                    dve.wait(t, core.ev["exp turned", j % 2])
                    t = dve.done(dve.eng.scalar_tensor_tensor(e, z, -1.0, z, ALU.mult, ALU.min))
                    act.wait(t)
                    t = act.done(act.eng.activation(e, e, ACT.Exp))
                    act.wait(t)
                    t = act.done(act.eng.activation(e, e, ACT.Ln, bias=1.0))
                    dve.wait(t, s_free[j])
                    t = core.ev["exp turned", j % 2] = spt[j] = dve.done(dve.eng.scalar_tensor_tensor(s, z, 0.0, e, ALU.max, ALU.add))
                for j in range(3, -1, -1):
                    w, rb = T - P * j, 4 + j % 2
                    pe.wait(core.ev["bank read", rb], *spt.values())
                    ins = pe.eng.matmul(core.bank[rb][:, 0:w], const(core, "tri_from"), sp_[j][:, 0:w], start=True, stop=j == 3)
                    for jj in range(j + 1, 4):
                        ins = pe.eng.matmul(core.bank[rb][:, P * (jj - j):w], const(core, "ones"), sp_[jj][:, 0:T - P * jj],
                                            start=False, stop=jj == 3)
                    t = pe.done(ins)
                    for jj in range(j, 4):
                        s_free[jj] = t
                    dve.wait(t)
                    t = core.ev["bank read", rb] = dve.done(dve.eng.tensor_tensor(zs[j][:, 0:w], zs[j][:, 0:w], core.bank[rb][:, 0:w], ALU.subtract))
                    act.wait(t)
                    at[j] = act.done(act.eng.activation(zs[j][:, 0:w], zs[j][:, 0:w], ACT.Exp))
                pe.wait(core.ev["bank read", 6], *at.values())
                for b in range(NB):
                    for j in range(b + 1):
                        ins = pe.eng.matmul(core.bank[6][:, b * HD:(b + 1) * HD], zs[j][:, P * (b - j):P * (b - j + 1)],
                                            vb[:, j, bass.ds(m * P + a * HD, HD)], start=j == 0, stop=j == b)
                t = pe.done(ins)
                z_free = [t] * 4
                dve.wait(t)
                core.ev["bank read", 6] = core.ev["heads written"] = dve.done(dve.eng.tensor_copy(
                    core.on[:, :, r], core.bank[6][:, 0:NB * HD].rearrange("p (b d) -> p b d", d=HD)))
            head_norm(core, sq, core.on, 2 * NB, HD, vec(core, "sb_g").unsqueeze(1).to_broadcast([P, 2 * NB, HD]))
            store_heads(core, m + 4, (core.ev["heads written"],))
            barrier(core)
    add_projection(core, CH_2O)


def difference(core, b, n0, n1, note0, note1, lam):
    def stage():
        dve, w = core.dve, P * (b + 1)
        inv = core.small[:, 128 + 2 * b:130 + 2 * b]
        dve.wait(note0["exp"], note1["exp"])
        dve.done(dve.eng.reciprocal(inv[:, 0:1], note0["total"]))
        t = dve.done(dve.eng.reciprocal(inv[:, 1:2], note1["total"]))
        dve.wait(t)
        t = dve.done(dve.eng.tensor_tensor(inv[:, 1:2], inv[:, 1:2], lam[:, 3:4], ALU.mult))
        dve.wait(t)
        t = dve.done(dve.eng.tensor_scalar(note1["e"][:, 0:w], note1["e"][:, 0:w], inv[:, 1:2], None, ALU.mult))
        dve.wait(t)
        t = dve.done(dve.eng.scalar_tensor_tensor(note0["e"][:, 0:w], note0["e"][:, 0:w], inv[:, 0:1], note1["e"][:, 0:w],
                                                  ALU.mult, ALU.subtract))
        core.ev["exp turned", n1 % 3] = t
        note0["diff"], note0["slot"] = t, n0 % 3
    return stage


def plain(core, b):
    def finish(product, tick, ob):
        core.dve.wait(tick)
        core.ev["heads written"] = core.ev["bank read", ob] = core.dve.done(core.dve.eng.tensor_copy(core.on[:, b, :], product))
    return finish


def head_norm(core, sq, o, n, width, gain):
    act, dve = core.act, core.dve
    st = core.small[:, 320:320 + n]
    ov = o.rearrange("p b d -> p (b d)").rearrange("p (n w) -> p n w", w=width)
    sv = sq.rearrange("p b d -> p (b d)").rearrange("p (n w) -> p n w", w=width)
    act.wait(core.ev["heads written"])
    t = act.done(act.eng.activation(sq, o, ACT.Square))
    dve.wait(t)
    t = dve.done(dve.eng.tensor_reduce(st, sv, AX.X, ALU.add))
    _, t = inverse_root(core, st, st, width, t)
    dve.wait(t)
    t = dve.done(dve.eng.tensor_tensor(ov, ov, st.unsqueeze(2).to_broadcast([P, n, width]), ALU.mult))
    dve.wait(t)
    core.ev["heads written"] = dve.done(dve.eng.tensor_tensor(ov, ov, gain, ALU.mult))


def dump_x(core):
    s = sem(core, "dumped")
    core.sp.eng.dma_start(core.out, core.x).then_inc(s, 16)
    core.sp.eng.wait_ge(s, 16)


def moe(core):
    nc, pe, act, dve, pool, sp = core.nc, core.pe, core.act, core.dve, core.pool, core.sp
    core.dense.close()
    st = core.stack
    half = KT * EH // 2
    core.w = [{(n, h): landing(core, f"{n}_{q}{h}", [P, half], st) for n in ("e1", "e3", "e2") for h in range(2)}
              for q in range(2)]
    for q in range(2):
        for key in core.w[q]:
            load_expert(core, q, key, q)
    norm(core, "g_ffn", core.u)
    core.hscr = nc.dram_tensor("h_tokens", [T, D], F32, kind="Internal").ap()
    core.yscr = nc.dram_tensor("y_pairs", [2 * T, D], F32, kind="Internal").ap()
    core.meta = sb(core, "meta", [P, NB, NE, 4])
    core.pos = sb(core, "pos", [P, NB, NE])
    core.S = sb(core, "slot_onehot", [P, NB, P])
    core.xg = sb(core, "xg", [P, D])
    core.xT = [sb(core, f"xT{q}", [P, KT, P]) for q in range(2)]
    core.hN = sb(core, "hN", [P, EH])
    core.sig = sb(core, "sig", [P, EH])
    core.hT = sb(core, "hT", [P, EH // P, P])
    core.oN = [sb(core, f"oN{j}", [P, D]) for j in range(SETS)]
    core.mt = [sb(core, f"mt{j}", [P, 4]) for j in range(SETS)]
    core.idx = [sb(core, f"idx{j}", [P, 2], I32) for j in range(SETS)]
    core.gathered, core.scattered = sem(core, "gathered"), [sem(core, f"scattered{j}") for j in range(SETS)]
    core.idx_ready, core.o_ready = sem(core, "idx_ready"), sem(core, "o_ready")
    core.slot_out = sb(core, "slot_out", [P, 1])
    count = sb(core, "count", [P, 2], I32)
    route(core, count)
    dve.done(dve.eng.memset(core.xg, 0.0))
    barrier(core)
    dispatch(core, 0, 0, 0, 0)()
    for h in range(2):
        turn(core, 0, 0, h)
    for e in range(2):
        expert(core, e, e, 0, e + 1, refill=e + 2)
    barrier(core, pool=False)
    with nc.Fori(0, (NE - 4) // SETS) as i:
        for s in range(2, 2 + SETS):
            expert(core, s % SETS, i * SETS + s, i + s // SETS, i * SETS + (s + 1), refill=i * SETS + (s + 2))
        barrier(core, pool=False)
    expert(core, SETS - 2, NE - 2, NE // SETS - 1, NE - 1)
    expert(core, SETS - 1, NE - 1, NE // SETS - 1, None, prior=(core.scattered[SETS - 2], NE // SETS * 16))
    for j in range(SETS):
        pool.eng.wait_ge(core.scattered[j], NE // SETS * 16)
    barrier(core)
    most = nc.values_load(count[0:1, 0:1], min_val=0, max_val=T)
    with nc.If(most > CAP):
        with nc.Fori(0, NE) as e:
            with nc.Fori(1, T // CAP) as c:
                for key in core.w[0]:
                    load_expert(core, 0, key, e)
                extra = e * (T // CAP - 1) + (c - 1)
                rounds = extra + NE // SETS
                dispatch(core, 0, e, c, rounds)()
                for h in range(2):
                    turn(core, 0, extra + NE, h)
                expert(core, 0, extra + NE, rounds, None)
                core.pool.eng.wait_ge(core.scattered[0], rounds * 16 + 16)
                core.pool.eng.sem_inc(core.pool.sem, 1)
                core.pool.n += 1
                barrier(core)
    nc.end_ifs()
    barrier(core)
    add_choices(core)


def load_expert(core, q, key, e, *used):
    name, h = key
    w = core.t[name][e:e + 1] if isinstance(e, int) else core.t[name][bass.ds(e, 1)]
    n = core.w[q][key].ap.shape[1]
    core.w[q][key].load(core.sp, w[:, :, h * n:(h + 1) * n].rearrange("o p n -> p (o n)"), *used)


def first_of_equals(core, onehot, values, best, tmp, mr, n):
    dve = core.dve
    bc = lambda v: v.unsqueeze(2).to_broadcast([P, NB, n])
    t = dve.done(dve.eng.tensor_tensor(tmp, values, bc(best), ALU.is_equal))
    dve.wait(t)
    t = dve.done(dve.eng.tensor_tensor(tmp, tmp, const(core, "rev8")[:, 0:n].unsqueeze(1).to_broadcast([P, NB, n]), ALU.mult))
    dve.wait(t)
    t = dve.done(dve.eng.tensor_reduce(mr, tmp, AX.X, ALU.max))
    dve.wait(t)
    t = dve.done(dve.eng.tensor_tensor(onehot, tmp, bc(mr), ALU.is_equal))
    dve.wait(t)


def route(core, count):
    pe, act, dve = core.pe, core.act, core.dve
    with ExitStack() as st:
        wr = landing(core, "w_router", [P, KT, NG + NE], st)
        wr.load(core.sp, core.t["router"])
        stage = core.oN[0:2]
        stored = [sem(core, f"h_stored{q}") for q in range(2)]
        for b in range(NB):
            for h in range(2):
                bank = 4 + 2 * (b % 2) + h
                pe.wait(core.ev["bank read", bank])
                for k in range(4):
                    ins = pe.eng.transpose(core.bank[bank][:, k * P:(k + 1) * P], core.u[:, 4 * h + k, b * P:(b + 1) * P], const(core, "ident"))
                t = pe.done(ins)
                e = (act, dve)[h]
                e.wait(t)
                if b >= 2:
                    e.eng.wait_ge(stored[b % 2], 16 * (b // 2))
                copy = e.eng.tensor_copy if h else e.eng.copy
                t = core.ev["bank read", bank] = e.done(copy(stage[b % 2][:, h * T:(h + 1) * T], core.bank[bank]))
                core.sp.wait(t)
            core.sp.eng.dma_start(core.hscr[b * P:(b + 1) * P, :], stage[b % 2]).then_inc(stored[b % 2], 16)
        wr.wait(pe)
        n = NG + NE
        pe.wait(core.ev["bank read", 0])
        for b in range(NB):
            for k in range(KT):
                ins = pe.eng.matmul(core.bank[0][:, b * n:(b + 1) * n], core.u[:, k, b * P:(b + 1) * P], wr.ap[:, k, :],
                                    start=k == 0, stop=k == KT - 1)
        t = pe.done(ins)
        lg = sb(core, "logits", [P, NB, n], stack=st)
        dve.wait(t)
        t = core.ev["bank read", 0] = dve.done(dve.eng.tensor_tensor(
            lg, core.bank[0][:, 0:NB * n].rearrange("p (b n) -> p b n", n=n),
            vec(core, "b_router").unsqueeze(1).to_broadcast([P, NB, n]), ALU.add))
        dve.wait(t)
        g, e4 = lg[:, :, 0:NG], lg[:, :, NG:].rearrange("p b (g e) -> p b g e", e=EPG)
        col = lambda name: sb(core, name, [P, NB], stack=st)
        gm, gs, m1, m2, sm, mr, g1, g2 = (col(f"col{j}") for j in range(8))
        oh = sb(core, "group", [P, NB, NG], stack=st)
        eg = sb(core, "group_exp", [P, NB, NG], stack=st)
        tmp4 = sb(core, "tmp4", [P, NB, NG], stack=st)
        tmp8, pr, oh1, oh2, p2 = (sb(core, f"eight{j}", [P, NB, EPG], stack=st) for j in range(5))
        big, a1, a2, m = (sb(core, f"assign{j}", [P, NB, NG, EPG], stack=st) for j in range(4))

        def step(ins):
            dve.wait(dve.done(ins))
        step(dve.eng.tensor_reduce(gm, g, AX.X, ALU.max))
        first_of_equals(core, oh, g, gm, tmp4, mr, NG)
        bc = lambda v, k: v.unsqueeze(2).to_broadcast([P, NB, k])
        t = dve.done(dve.eng.tensor_tensor(eg, g, bc(gm, NG), ALU.subtract))
        act.wait(t)
        dve.wait(act.done(act.eng.activation(eg, eg, ACT.Exp)))
        step(dve.eng.tensor_reduce(gs, eg, AX.X, ALU.add))
        step(dve.eng.reciprocal(gs, gs))
        g8 = lambda v: v.unsqueeze(3).to_broadcast([P, NB, NG, EPG])
        e8 = lambda v: v.unsqueeze(2).to_broadcast([P, NB, NG, EPG])
        step(dve.eng.tensor_tensor(big, e4, g8(oh), ALU.mult))
        step(dve.eng.tensor_reduce(pr, big.rearrange("p b g e -> p b e g"), AX.X, ALU.add))
        step(dve.eng.tensor_reduce(m1, pr, AX.X, ALU.max))
        t = dve.done(dve.eng.tensor_tensor(pr, pr, bc(m1, EPG), ALU.subtract))
        act.wait(t)
        dve.wait(act.done(act.eng.activation(pr, pr, ACT.Exp)))
        step(dve.eng.tensor_reduce(sm, pr, AX.X, ALU.add))
        step(dve.eng.reciprocal(sm, sm))
        step(dve.eng.tensor_tensor(pr, pr, bc(sm, EPG), ALU.mult))
        step(dve.eng.tensor_reduce(m1, pr, AX.X, ALU.max))
        first_of_equals(core, oh1, pr, m1, tmp8, mr, EPG)
        step(dve.eng.scalar_tensor_tensor(p2, oh1, -2.0, pr, ALU.mult, ALU.add))
        step(dve.eng.tensor_reduce(m2, p2, AX.X, ALU.max))
        first_of_equals(core, oh2, p2, m2, tmp8, mr, EPG)
        step(dve.eng.tensor_tensor(sm, m1, m2, ALU.add))
        step(dve.eng.reciprocal(sm, sm))
        step(dve.eng.tensor_tensor(sm, sm, gs, ALU.mult))
        step(dve.eng.tensor_tensor(g1, m1, sm, ALU.mult))
        step(dve.eng.tensor_tensor(g2, m2, sm, ALU.mult))
        for a, o in ((a1, oh1), (a2, oh2)):
            step(dve.eng.tensor_copy(big, g8(oh)))
            step(dve.eng.tensor_tensor(a, big, e8(o), ALU.mult))
        step(dve.eng.tensor_tensor(m, a1, a2, ALU.add))
        flat = lambda v: v.rearrange("p b g e -> p b (g e)")
        tok = const(core, "token").unsqueeze(2).to_broadcast([P, NB, NE])
        step(dve.eng.tensor_copy(core.meta[:, :, :, 0], tok))
        step(dve.eng.scalar_tensor_tensor(flat(big), tok, 2.0, flat(a2), ALU.mult, ALU.add))
        step(dve.eng.tensor_copy(core.meta[:, :, :, 1], flat(big)))
        step(dve.eng.tensor_tensor(flat(a1), flat(a1), bc(g1, NE), ALU.mult))
        step(dve.eng.tensor_tensor(flat(a2), flat(a2), bc(g2, NE), ALU.mult))
        step(dve.eng.tensor_tensor(core.meta[:, :, :, 2], flat(a1), flat(a2), ALU.add))
        step(dve.eng.memset(core.meta[:, :, :, 3], 1.0))
        mf = flat(m)
        pe.wait((dve.sem, dve.n))
        for b in range(NB):
            ins = pe.eng.matmul(core.bank[1][:, b * NE:(b + 1) * NE], const(core, "tri_before"), mf[:, b, :], start=True, stop=b == 0)
            for j in range(b):
                ins = pe.eng.matmul(core.bank[1][:, b * NE:(b + 1) * NE], const(core, "ones"), mf[:, j, :], start=False, stop=j == b - 1)
        for b in range(NB):
            ins = pe.eng.matmul(core.bank[2][:, 0:NE], const(core, "ones"), mf[:, b, :], start=b == 0, stop=b == NB - 1)
        dve.wait(pe.done(ins))
        step(dve.eng.tensor_tensor(core.pos, mf, core.bank[1][:, 0:NB * NE].rearrange("p (b e) -> p b e", e=NE), ALU.mult))
        step(dve.eng.tensor_tensor(core.pos, core.pos, mf, ALU.add))
        step(dve.eng.tensor_scalar(core.pos, core.pos, -1.0, None, ALU.add))
        step(dve.eng.tensor_reduce(gm[:, 0:1], core.bank[2][:, 0:NE], AX.X, ALU.max))
        step(dve.eng.tensor_copy(count[:, 0:1], gm[:, 0:1]))
        dve.done(dve.eng.memset(core.slot_out, float(4 * T)))
        for q in range(2):
            core.pool.eng.wait_ge(stored[q], 32)
            core.sp.eng.wait_ge(stored[q], 32)
        barrier(core)


def dispatch(core, j, e, c, rounds):
    pe, dve, pool = core.pe, core.dve, core.pool
    iota = const(core, "iota")[:, c * CAP:(c + 1) * CAP] if isinstance(c, int) else const(core, "iota")[:, bass.ds(c * CAP, CAP)]
    at = slice(e, e + 1) if isinstance(e, int) else bass.ds(e, 1)
    dve.wait(core.ev["S used"])
    for b in range(NB):
        slots = dve.done(dve.eng.tensor_scalar(core.S[:, b, :], iota, core.pos[:, b, at], None, ALU.is_equal))

    def rest():
        pe.wait(slots, core.ev["bank read", 7])
        for b in range(NB):
            ins = pe.eng.matmul(core.bank[7][:, 0:4], core.S[:, b, :], core.meta[:, b, at, :].rearrange("p o c -> p (o c)"),
                                start=b == 0, stop=b == NB - 1)
        t = core.ev["S used"] = pe.done(ins)
        dve.wait(t)
        dve.eng.wait_ge(core.scattered[j], rounds * 16)
        mt, idx = core.mt[j], core.idx[j]
        t = core.ev["bank read", 7] = dve.done(dve.eng.tensor_copy(mt, core.bank[7][:, 0:4]))
        dve.wait(t)
        t = dve.done(dve.eng.tensor_scalar(mt[:, 3:4], mt[:, 3:4], -4.0 * T, 4.0 * T, ALU.mult, ALU.add))
        dve.wait(t)
        dve.eng.tensor_scalar(idx, mt[:, 0:2], mt[:, 3:4], None, ALU.add).then_inc(core.idx_ready, 1)
        pool.eng.wait_ge(core.idx_ready, 1)
        pool.eng.sem_clear(core.idx_ready)
        pool.eng.indirect_dma_start(core.xg, None, core.hscr, bass.IndirectOffsetOnAxis(ap=idx[:, 0:1].bitcast(U32), axis=0),
                                    bounds_check=T - 1, oob_is_err=False).then_inc(core.gathered, 16)
    return rest


def turn(core, q, block, h):
    pe = core.pe
    if h == 0:
        pe.eng.wait_ge(core.gathered, block * 16 + 16)
    pe.wait(core.ev["bank read", h])
    for k in range(4):
        kk = 4 * h + k
        ins = pe.eng.transpose(core.bank[h][:, k * P:(k + 1) * P], core.xg[:, kk * P:(kk + 1) * P], const(core, "ident"))
    t = pe.done(ins)
    e = (core.act, core.dve)[h]
    e.wait(t, core.ev["xT used", q])
    copy = e.eng.tensor_copy if h else e.eng.copy
    core.ev["bank read", h] = core.ev["xT written", h] = e.done(
        copy(core.xT[q][:, 4 * h:4 * h + 4, :].rearrange("p k t -> p (k t)"), core.bank[h]))


def expert(core, j, block, rounds, nxt, refill=None, prior=None):
    pe, act, dve, pool = core.pe, core.act, core.dve, core.pool
    q, after = j % 2, (j + 1) % SETS
    w, xT = core.w[q], core.xT[q]
    if nxt is not None:
        rest = dispatch(core, after, nxt, 0, rounds + 1 if after == 0 else rounds)

    def product(bank, name):
        pe.wait(core.ev["bank read", bank])
        for h in range(2):
            pe.wait(core.ev["xT written", h])
            w[name, h].wait(pe)
            for k in range(4):
                ins = pe.eng.matmul(core.bank[bank], xT[:, 4 * h + k, :], w[name, h].ap[:, k * EH:(k + 1) * EH],
                                    start=h + k == 0, stop=h == 1 and k == 3)
            t = pe.done(ins)
            if refill is not None:
                load_expert(core, q, (name, h), refill, t)
        return t
    t = product(2, "e1")
    act.wait(t, core.ev["hN turned"])
    t1 = act.done(act.eng.activation(core.sig, core.bank[2], ACT.Exp, scale=-1.0))
    if nxt is not None:
        rest()
    dve.wait(t1)
    dve.wait(dve.done(dve.eng.tensor_scalar(core.sig, core.sig, 1.0, None, ALU.add)))
    dve.wait(dve.done(dve.eng.reciprocal(core.sig, core.sig)))
    t1 = core.ev["bank read", 2] = dve.done(dve.eng.tensor_tensor(core.sig, core.sig, core.bank[2], ALU.mult))
    t = core.ev["xT used", q] = product(3, "e3")
    dve.wait(t, t1)
    th = core.ev["bank read", 3] = dve.done(dve.eng.tensor_tensor(core.hN, core.sig, core.bank[3], ALU.mult))
    if nxt is not None:
        turn(core, 1 - q, block + 1, 0)
    pe.wait(th, core.ev["bank read", 4])
    for k in range(EH // P):
        ins = pe.eng.transpose(core.bank[4][:, k * P:(k + 1) * P], core.hN[:, k * P:(k + 1) * P], const(core, "ident"))
    t = core.ev["hN turned"] = pe.done(ins)
    act.wait(t, core.ev["hT used"])
    t = core.ev["bank read", 4] = act.done(act.eng.copy(core.hT.rearrange("p k t -> p (k t)"), core.bank[4]))
    if nxt is not None:
        turn(core, 1 - q, block + 1, 1)
    pe.wait(t)
    for h in range(2):
        w["e2", h].wait(pe)
        for k in range(2):
            for n in range(2):
                ins = pe.eng.matmul(core.bank[5 + n], core.hT[:, 2 * h + k, :], w["e2", h].ap[:, k * D + n * T:k * D + (n + 1) * T],
                                    start=h + k == 0, stop=h == 1 and k == 1)
        t = pe.done(ins)
        if refill is not None:
            load_expert(core, q, ("e2", h), refill, t)
    core.ev["hT used"] = t
    gate, o = core.mt[j][:, 2:3], core.oN[j]
    act.wait(t, prior)
    act.eng.wait_ge(core.scattered[j], rounds * 16)
    act.eng.activation(o[:, 0:T], core.bank[5], ACT.Copy, scale=gate).then_inc(core.o_ready, 1)
    dve.wait(t, prior)
    dve.eng.wait_ge(core.scattered[j], rounds * 16)
    dve.eng.tensor_scalar(o[:, T:], core.bank[6], gate, None, ALU.mult).then_inc(core.o_ready, 1)
    pool.eng.wait_ge(core.o_ready, 2)
    pool.eng.sem_clear(core.o_ready)
    pool.eng.indirect_dma_start(core.yscr, bass.IndirectOffsetOnAxis(ap=core.idx[j][:, 1:2].bitcast(U32), axis=0), o, None,
                                bounds_check=2 * T - 1, oob_is_err=False).then_inc(core.scattered[j], 16)


def add_choices(core):
    pe, act, dve, sp = core.pe, core.act, core.dve, core.sp
    pairs = [Landing(core.u[:, 4 * q:4 * q + 4, :].rearrange("p k t -> p (k t)"), sem(core, f"pairs{q}")) for q in range(2)]
    outs = [core.oN[q] for q in range(2)]
    out_sem = [sem(core, f"out{q}") for q in range(2)]
    y = core.yscr.rearrange("(t c) d -> t (c d)", c=2)
    used = [None, None]
    for b in range(NB):
        q = b % 2
        pairs[q].load(sp, y[b * P:(b + 1) * P, :], used[q])
        pr = pairs[q].ap
        pairs[q].wait(dve)
        if b >= 2:
            dve.eng.wait_ge(out_sem[q], 16)
        t = dve.done(dve.eng.tensor_tensor(outs[q], pr[:, 0:D], pr[:, D:], ALU.add))
        used[q] = t
        dve.wait(t)
        for h in range(2):
            bank = 2 * q + h
            pe.wait(core.ev["bank read", bank])
            for k in range(4):
                ins = pe.eng.transpose(core.bank[bank][:, k * P:(k + 1) * P], core.x[:, 4 * h + k, b * P:(b + 1) * P], const(core, "ident"))
            dve.wait(pe.done(ins))
            o = outs[q][:, h * T:(h + 1) * T]
            t = core.ev["bank read", bank] = dve.done(dve.eng.tensor_tensor(o, o, core.bank[bank], ALU.add))
        act.wait(t)
        act.eng.dma_start(core.out[b * P:(b + 1) * P, :], outs[q]).then_inc(out_sem[q], 16)
    for q in range(2):
        sp.eng.wait_ge(out_sem[q], 32)


def kernel(**inputs):
    import concourse.bacc as bacc
    from concourse.bass_utils import run_bass_kernel_spmd

    arrays, vpack = lay_out({n: np.asarray(a) for n, a in inputs.items()})
    cpack = Packed(shape_constants())
    arrays["consts"], arrays["vecs"] = cpack.array, vpack.array
    arrays = {n: np.ascontiguousarray(a) for n, a in arrays.items()}
    nc = bacc.Bacc("TRN2", target_bir_lowering=False, num_devices=1)
    t = {n: nc.dram_tensor("in_" + n, a.shape, mybir.dt.from_np(a.dtype), kind="ExternalInput").ap() for n, a in arrays.items()}
    out = nc.dram_tensor("out", [T, D], F32, kind="ExternalOutput").ap()
    program(nc, t, cpack, vpack, out)
    r = run_bass_kernel_spmd(nc, [{"in_" + n: a for n, a in arrays.items()}], core_ids=[0])
    return r.results[0]["out"].reshape(1, T, D)
```

```python
from contextlib import ExitStack

import numpy as np

import concourse.bass as bass
from concourse import mybir
from concourse.alu_op_type import AluOpType as ALU

F32 = mybir.dt.float32
I32 = mybir.dt.int32
U32 = mybir.dt.uint32
ACT = mybir.ActivationFunctionType
AX = mybir.AxisListType

P = 128
T = 512
D = 1024
KT = D // P
NB = T // P
D_FF = 4096
FT = D_FF // P
EPS = 1e-6
NEG = -1e30
TAKEN = -3e38
RING = 8
HD = 64
SCALE = HD ** -0.5
ROPE = 16
TOPK = 128
N_CMP, CMP_LEN, CMP_STRIDE = 31, 32, 16
NE, NG, EPG = 32, 4, 8
EH = 512
CAP = 128
SETS = 4
BUCKETS = 32
LV = 640
LAMBDA_INIT = 0.8 - 0.6

N_AB, N_C, N_2, N_O = 24, 16, 24, 8
CH_AB = 0
CH_ABO = CH_AB + N_AB
CH_M0 = CH_ABO + N_O
CH_C = CH_M0 + 2 * FT
CH_CO = CH_C + N_C
CH_M1 = CH_CO + N_O
CH_2 = CH_M1 + 2 * FT
CH_2O = CH_2 + N_2
N_CH = CH_2O + N_O


def shape_constants():
    p = np.arange(P)
    f = np.float32
    c = {}
    c["ident"] = np.eye(P)
    c["ones"] = np.ones((P, P))
    c["pair_ones"] = (p[:, None] // HD == p[None, :] // HD)
    swap = np.zeros((P, P))
    for r in range(P):
        if r % HD < ROPE // 2:
            swap[r + ROPE // 2, r] = -1.0
        elif r % HD < ROPE:
            swap[r - ROPE // 2, r] = 1.0
    c["swap"] = swap
    sel = np.zeros((P, P))
    for r in range(ROPE):
        sel[HD + r, r] = sel[HD + r, HD + r] = 1.0
    c["sel_rope"] = sel
    dup = np.zeros((P, P))
    for r in range(HD):
        dup[r, r] = dup[r, HD + r] = 1.0
    c["dup"] = dup
    inv = (f(500000.0) ** (-np.arange(0, ROPE, 2, dtype=f) / f(ROPE))).astype(f)
    ang = np.arange(T, dtype=f)[:, None] * inv[None, :]
    cos, sin = np.cos(ang).T, np.sin(ang).T
    rc, rs = np.ones((P, T)), np.zeros((P, T))
    for r in range(P):
        if r % HD < ROPE:
            rc[r], rs[r] = cos[r % HD % (ROPE // 2)], sin[r % HD % (ROPE // 2)]
    c["rope_c"], c["rope_s"] = rc, rs
    c["rope_cq"], c["rope_sq"] = rc * SCALE, rs * SCALE
    k = np.arange(T)[None, :] - (T - P)
    c["causal"] = np.where(k <= p[:, None], 0.0, NEG)
    c["chunked"] = np.where(k // HD <= p[:, None] // HD, 0.0, NEG)
    c["strict"] = np.where(p[:, None] < p[None, :], 0.0, NEG)
    c["tri_from"] = (p[:, None] >= p[None, :])
    c["tri_before"] = (p[:, None] < p[None, :])
    n = np.arange(32)
    t = np.arange(NB)[None, :, None] * P + p[:, None, None]
    ok = (n[None, None, :] < N_CMP) & (n[None, None, :] * CMP_STRIDE + CMP_LEN - 1 <= t)
    ok = np.repeat(ok[:, :, None, :], 2, axis=2)
    c["cmp_add"] = np.where(ok, 0.0, NEG).reshape(P, -1)
    c["cmp_one"] = ok.reshape(P, -1)
    rel = np.arange(LV) - (T - 1)
    half, exact = BUCKETS // 2, BUCKETS // 4
    m = np.abs(rel)
    mf = np.maximum(m, 1).astype(f)
    large = exact + (np.log(mf / f(exact)) / f(np.log(128 / exact)) * f(half - exact)).astype(np.int32)
    bucket = np.where(rel > 0, half, 0) + np.where(m < exact, m, np.minimum(large, half - 1))
    oh = np.zeros((P, LV))
    oh[bucket, np.arange(LV)] = 1.0
    c["buckets"] = oh
    c["iota"] = np.broadcast_to(np.arange(T), (P, T))
    c["rev8"] = np.broadcast_to(8.0 - np.arange(8), (P, 8))
    c["token"] = np.arange(NB)[None, :] * P + p[:, None]
    c["slot"] = p[:, None]
    return {n: np.ascontiguousarray(a, dtype=f) for n, a in c.items()}


class Packed:

    def __init__(self, parts):
        self.at, w = {}, 0
        for name, a in parts.items():
            self.at[name] = (w, a.shape[1])
            w += a.shape[1]
        self.width = w
        self.array = np.concatenate(list(parts.values()), axis=1)

    def view(self, ap, name):
        o, w = self.at[name]
        return ap[:, o:o + w]


def chunks(w):
    k, n = w.shape
    a = w.reshape(k // D, KT, P, n // P, P)
    return a.transpose(3, 0, 2, 1, 4).reshape(-1, P, KT * P)


def columns(w, cols):
    out = np.zeros((w.shape[0], len(cols)), w.dtype)
    cols = np.asarray(cols)
    out[:, cols >= 0] = w[:, cols[cols >= 0]]
    return out


def lay_out(i):
    a = {}
    ab, cw, w2 = i["ab_w_in"][0], i["c_w_in"][0], i["w_in_2"][0]
    r = lambda o, n: list(range(o, o + n))
    pad = lambda n: [-1] * n
    aq, ckv, akr, aqi, aki, awi, bq, bk, bv, bf = np.cumsum([0, 512, 256, 16, 512, 64, 8, 512, 512, 512])
    cols = (r(aq, 512) + r(aqi, 512) + r(bq, 512) + r(bk, 512) + r(ckv, 256)
            + r(aki, 64) + r(akr, 16) + pad(48) + r(bf, 8) + pad(24) + r(awi, 8) + pad(88) + r(bv, 512))
    s_ab = chunks(columns(ab, cols))
    heads = [h for m in range(8) for h in (m, m + 8)]
    q_cols = [h * HD + d for h in heads for d in range(HD)]
    o = [D + 128 * j for j in range(7)]
    gate_cols = [o[6] + h * 3 + b for h in heads for b in range(3)]
    cols = (q_cols + r(o[0], 128) + r(o[2], 128) + r(o[4], 128) + r(o[1], 128) + r(o[3], 128) + r(o[5], 128)
            + gate_cols + pad(80) + pad(128))
    s_c = chunks(columns(cw, cols))
    ml = lambda l: [chunks(i["mlp_w1"][l]), chunks(i["mlp_w2"][l])]
    a["dense"] = np.concatenate([s_ab, chunks(i["ab_w_out"][0])] + ml(0)
                                + [s_c, chunks(i["c_w_out"][0][q_cols])] + ml(1)
                                + [chunks(w2), chunks(i["w_o_2"][0])])
    a["xT"] = i["x"][0].T.reshape(KT, P, T).transpose(1, 0, 2)
    tiles = lambda w: w.reshape(-1, P, w.shape[1]).transpose(1, 0, 2)
    uk = i["a_w_uk"][0]
    ukp = np.zeros((256, 8, HD), np.float32)
    ukp[:, :, ROPE:] = uk
    a["w_uk"] = tiles(ukp.reshape(256, 512))
    a["w_uv"] = tiles(i["a_w_uv"][0].reshape(256, 512))
    for n in "kv":
        w = i[f"c_cmp_{n}_w1"][0].reshape(CMP_LEN, HD, P).transpose(1, 0, 2)
        a[f"cmp_{n}1"] = np.concatenate([w, w], 0)
    k2 = np.zeros((P, 2, P), np.float32)
    k2[:, 0, :HD] = k2[:, 1, HD:] = i["c_cmp_k_w2"][0]
    a["cmp_k2"] = k2
    a["cmp_v2"] = i["c_cmp_v_w2"][0]
    a["router"] = tiles(np.concatenate([i["w_router_g_2"][0], i["w_router_e_2"][0]], 1))
    e1 = lambda w: w.reshape(NE, KT, P, EH).transpose(0, 2, 1, 3).reshape(NE, P, KT * EH)
    a["e1"], a["e3"] = e1(i["w1_2"][0]), e1(i["w3_2"][0])
    a["e2"] = i["w2_2"][0].reshape(NE, EH // P, P, D).transpose(0, 2, 1, 3).reshape(NE, P, -1)
    col = lambda v: v.reshape(-1, P).T
    row = lambda v: np.broadcast_to(v.reshape(1, -1), (P, v.size))
    short = lambda v: np.concatenate([v.reshape(-1, 1), np.zeros((P - v.size, 1), np.float32)], 0)
    twice = lambda v: np.concatenate([v, v], 0)
    rb = np.zeros((P, NG, P), np.float32)
    rb[:BUCKETS] = np.broadcast_to(i["rel_bias_2"][:, :, None], (BUCKETS, 4, P))
    vecs = {
        "g_a0": col(i["attn_norm"][0]), "g_a1": col(i["attn_norm"][1]), "g_m0": col(i["mlp_norm"][0]),
        "g_m1": col(i["mlp_norm"][1]), "g_fin": col(i["final_norm"]), "g_a2": col(i["g_attn_2"][0]),
        "g_ffn": col(i["g_ffn_2"][0]), "g_kv": col(i["a_kv_norm"][0]), "g_ki": short(i["a_kidx_norm"][0]),
        "b_f": short(i["ab_b_forget"][0]), "g_qn": twice(i["qn_g_2"][0][:, None]),
        "g_kn": twice(i["kn_g_2"][0][:, None]), "subln": col(i["subln_g_2"][0]), "sb_g": twice(i["sb_out_g_2"][0][:, None]),
        "b_gate": row(i["c_b_gate"][0].reshape(16, 3)[heads]),
        "b_router": row(np.concatenate([i["b_router_g_2"][0], i["b_router_e_2"][0]])),
        "lam": row(np.concatenate([i[f"lam_{n}_2"][0] for n in ("q1", "q2", "k1", "k2")])),
        "rel": rb.reshape(P, -1), "pe_k": twice(i["c_pe_k"][0].T), "pe_v": twice(i["c_pe_v"][0].T),
    }
    return a, Packed(vecs)


class Engine:

    def __init__(self, eng, sem):
        self.eng, self.sem, self.n = eng, sem, 0

    def done(self, ins):
        ins.then_inc(self.sem, 1)
        self.n += 1
        return self.sem, self.n

    def wait(self, *ticks):
        for t in ticks:
            if t is not None:
                self.eng.wait_ge(*t)


class Landing:

    def __init__(self, ap, sem):
        self.ap, self.sem = ap, sem

    def load(self, by, src, *released, dst=None):
        by.wait(*released)
        by.eng.dma_start(self.ap if dst is None else dst, src).then_inc(self.sem, 16)

    def wait(self, reader):
        reader.eng.wait_ge(self.sem, 16)
        reader.eng.sem_clear(self.sem)


class Events(dict):

    def __missing__(self, name):
        return None


class Core:

    def __init__(self):
        self.ev, self.names = Events(), 0




def program(nc, t, cpack, vpack, out, upto=None):
    core = Core()
    core.nc, core.t, core.cpack, core.vpack, core.out = nc, t, cpack, vpack, out
    with ExitStack() as stack:
        core.stack = stack
        begin(core)
        layer_ab(core)
        if upto != "a0":
            mlp(core, CH_M0, "g_m0")
        if upto not in ("a0", "m0"):
            layer_c(core)
        if upto not in ("a0", "m0", "a1"):
            mlp(core, CH_M1, "g_m1")
            norm(core, "g_fin", core.x, summed=True)
            barrier(core)
        if upto not in ("a0", "m0", "a1", "fn"):
            layer_2(core)
        if upto is not None:
            dump_x(core)
            return
        moe(core)


def sb(core, name, shape, dt=F32, stack=None):
    core.names += 1
    return (stack or core.stack).enter_context(core.nc.sbuf_tensor(f"{name}_{core.names}", shape, dt)).ap()


def sem(core, name):
    return core.stack.enter_context(core.nc.semaphore(name))


def landing(core, name, shape, stack=None, dt=F32):
    return Landing(sb(core, name, shape, dt, stack), sem(core, "landed_" + name))


def barrier(core, pool=True):
    for e in core.engines:
        if e.n:
            e.wait((e.sem, e.n))
    meet = [e for e in core.nc.engines if pool or e != mybir.EngineType.Pool]
    core.nc.multi_engine_barrier(meet, sems_to_clear=core.ticks)
    for e in core.engines:
        e.n = 0
    core.ev.clear()


def loop(core, n):
    barrier(core)
    return core.nc.Fori(0, n)


def const(core, name):
    return core.cpack.view(core.consts, name)


def vec(core, name):
    return core.vpack.view(core.vecs.ap, name)


def begin(core):
    nc, t = core.nc, core.t
    names = ["PE", "ACT", "DVE", "POOL", "SP"]
    sems = [sem(core, "tick_" + n) for n in names]
    assert [s.num for s in sems] == list(range(sems[0].num, sems[0].num + 5))
    core.ticks = range(sems[0].num, sems[0].num + 5)
    engs = [nc.tensor, nc.scalar, nc.vector, nc.gpsimd, nc.sync]
    core.engines = [Engine(e, s) for e, s in zip(engs, sems)]
    core.pe, core.act, core.dve, core.pool, core.sp = core.engines
    core.x = sb(core, "x", [P, KT, T])
    core.u = sb(core, "u", [P, KT, T])
    core.small = sb(core, "small", [P, 512])
    core.rs = sb(core, "rs", [P, T])
    core.sq = [sb(core, f"square{b}", [P, T]) for b in range(2)]
    core.eps = sb(core, "eps", [P, 1])
    core.bank = [core.stack.enter_context(nc.psum_tensor(f"bank{b}", [P, T], F32)).ap() for b in range(8)]
    core.free = [None] * 8
    core.vecs = landing(core, "vecs", [P, core.vpack.width])
    core.cland = landing(core, "consts", [P, core.cpack.width])
    core.consts = core.cland.ap
    core.dense = core.stack.enter_context(ExitStack())
    core.ring = [landing(core, f"ring{s}", [P, KT, P], core.dense) for s in range(RING)]
    xl = Landing(core.x, sem(core, "landed_x"))
    xl.load(core.sp, t["xT"])
    core.vecs.load(core.sp, t["vecs"])
    first, rest = slice(0, core.cpack.at["rope_c"][0]), slice(core.cpack.at["rope_c"][0], core.cpack.width)
    core.cland.load(core.sp, t["consts"][:, first], dst=core.consts[:, first])
    for s in range(RING):
        core.ring[s].load(core.sp, chunk(core, s))
    core.tables = sem(core, "landed_tables")
    core.sp.eng.dma_start(core.consts[:, rest], t["consts"][:, rest]).then_inc(core.tables, 16)
    for e in (core.pe, core.act, core.dve, core.pool):
        for l in (xl, core.cland, core.vecs):
            e.eng.wait_ge(l.sem, 16)
    core.dve.done(core.dve.eng.memset(core.eps, EPS))
    barrier(core)


def chunk(core, at):
    if isinstance(at, int):
        w = core.t["dense"][at:at + 1]
    else:
        w = core.t["dense"][bass.ds(at, 1)]
    return w.rearrange("o p (k m) -> p (o k) m", m=P)


def tile_products(core, slot, rhs, bank, start=True, stop=True, after=()):
    core.pe.wait(core.ev["bank read", bank] if start else None, *after)
    core.ring[slot].wait(core.pe)
    for k in range(KT):
        ins = core.pe.eng.matmul(core.bank[bank], core.ring[slot].ap[:, k, :], rhs(k),
                                 start=start and k == 0, stop=stop and k == KT - 1)
    return core.pe.done(ins)


def refill(core, slot, at, used):
    if at is None:
        return
    core.ring[slot].load(core.sp, chunk(core, at), used)


def evacuate(core, bank, dst, tick, n, after=()):
    e = (core.act, core.dve)[n % 2]
    e.wait(tick, *after)
    if n % 2:
        t = e.done(e.eng.tensor_copy(dst, core.bank[bank]))
    else:
        t = e.done(e.eng.copy(dst, core.bank[bank]))
    core.ev["bank read", bank] = t
    return t


def project(core, first, n, y):
    with loop(core, n // RING) as i:
        for j in range(RING):
            tick = tile_products(core, j, lambda k: core.u[:, k, :], j)
            refill(core, j, i * RING + (first + j + RING), tick)
            evacuate(core, j, y[:, bass.ds(i * RING + j, 1), :].rearrange("p o t -> p (o t)"), tick, j)
        barrier(core)


def square_in(core, xk, k, written):
    sq = core.sq[k % 2]
    core.act.wait(written, core.ev["square added", k % 2])
    t = core.act.done(core.act.eng.activation(sq, xk, ACT.Square))
    core.dve.wait(t, core.ev["square added"])
    core.ev["square added"] = core.ev["square added", k % 2] = core.dve.done(
        core.dve.eng.tensor_tensor(core.rs, core.rs, sq, ALU.add))


def add_projection(core, first, ready=()):
    core.ev["square added"] = core.dve.done(core.dve.eng.memset(core.rs, 0.0))
    for j in range(N_O):
        tick = tile_products(core, j, lambda k: core.u[:, k, :], j, after=ready)
        nxt = first + j + RING
        refill(core, j, nxt if nxt < N_CH else None, tick)
        core.dve.wait(tick)
        core.ev["bank read", j] = core.dve.done(core.dve.eng.tensor_tensor(
            core.x[:, j, :], core.x[:, j, :], core.bank[j], ALU.add))
        square_in(core, core.x[:, j, :], j, core.ev["bank read", j])
    barrier(core)


def sum_squares(core, tiles, weights, bank, after=()):
    for k, src in enumerate(tiles):
        sq = core.sq[k % 2]
        core.act.wait(core.ev["square summed", k % 2], *after)
        t = core.act.done(core.act.eng.activation(sq, src, ACT.Square))
        core.pe.wait(t, core.ev["bank read", bank] if k == 0 else None)
        core.ev["square summed", k % 2] = core.pe.done(core.pe.eng.matmul(
            core.bank[bank], weights, sq, start=k == 0, stop=k == len(tiles) - 1))
    return core.ev["square summed", (len(tiles) - 1) % 2]


def inverse_root(core, dst, src, n, width_tick):
    core.act.wait(width_tick)
    t = core.act.done(core.act.eng.activation(dst, src, ACT.Ln, bias=core.eps[0:dst.shape[0]], scale=1.0 / n))
    core.act.wait(t)
    return t, core.act.done(core.act.eng.activation(dst, dst, ACT.Exp, scale=-0.5))


def norm(core, gain, dst, summed=False):
    if summed:
        core.pe.wait(core.ev["bank read", 7])
        tick = core.pe.done(core.pe.eng.matmul(core.bank[7], const(core, "ones"), core.rs, start=True, stop=True))
    else:
        tick = sum_squares(core, [core.x[:, k, :] for k in range(KT)], const(core, "ones"), 7)
    core.ev["bank read", 7], t = inverse_root(core, core.rs, core.bank[7], D, tick)
    core.dve.wait(t)
    for k in range(KT):
        core.dve.done(core.dve.eng.scalar_tensor_tensor(
            dst[:, k, :], core.x[:, k, :], vec(core, gain)[:, k:k + 1], core.rs, ALU.mult, ALU.mult))


def mlp(core, first, gain):
    norm(core, gain, core.u, summed=True)
    with ExitStack() as st:
        h = sb(core, "h", [P, FT, T], stack=st)
        r = [sb(core, f"relu{b}", [P, T], stack=st) for b in range(2)]
        body = 2 * RING
        with loop(core, FT // body) as i:
            used = [None, None]
            for j in range(body):
                bank = slot = j % RING
                tick = tile_products(core, slot, lambda k: core.u[:, k, :], bank)
                refill(core, slot, i * body + (first + j + RING), tick)
                core.act.wait(tick, used[j % 2])
                t = core.act.done(core.act.eng.activation(r[j % 2], core.bank[bank], ACT.Relu))
                core.ev["bank read", bank] = t
                core.dve.wait(t)
                used[j % 2] = core.dve.done(core.dve.eng.tensor_tensor(
                    tile(h, i * body + j), r[j % 2], r[j % 2], ALU.mult))
            barrier(core)
        dve = core.dve
        dve.done(dve.eng.memset(core.rs, 0.0))
        per = FT // KT
        with loop(core, FT // body) as i:
            for m in range(body // per):
                for q in range(per):
                    s = m * per + q
                    tick = tile_products(core, s % RING, lambda k: h[:, q * KT + k, :], m, start=q == 0, stop=q == per - 1)
                    refill(core, s % RING, i * body + (first + FT + s + RING), tick)
                core.dve.wait(tick)
                xm = tile(core.x, i * (body // per) + m)
                core.ev["bank read", m] = core.dve.done(core.dve.eng.tensor_tensor(xm, xm, core.bank[m], ALU.add))
                square_in(core, xm, m, core.ev["bank read", m])
            barrier(core)


def rope(core, dst, src, c, s, bank, tmp, ready=()):
    core.pe.wait(core.ev["bank read", bank], *ready)
    t = core.pe.done(core.pe.eng.matmul(core.bank[bank], const(core, "swap"), src, start=True, stop=True))
    core.dve.wait(*ready)
    core.dve.done(core.dve.eng.tensor_tensor(tmp[0], src, const(core, c), ALU.mult))
    core.dve.wait(t)
    t = core.ev["bank read", bank] = core.dve.done(core.dve.eng.tensor_tensor(tmp[1], core.bank[bank], const(core, s), ALU.mult))
    core.dve.wait(t)
    return core.dve.done(core.dve.eng.tensor_tensor(dst, tmp[0], tmp[1], ALU.add))


def tile(y, m):
    return y[:, bass.ds(m, 1), :].rearrange("p o t -> p (o t)")


def to_tokens(core, dst, tiles, after=()):
    for b in range(NB):
        bank = b % 4
        core.pe.wait(core.ev["bank read", bank], *after)
        for m, src in enumerate(tiles):
            ins = core.pe.eng.transpose(core.bank[bank][:, m * P:(m + 1) * P], src[:, b * P:(b + 1) * P], const(core, "ident"))
        t = core.pe.done(ins)
        e = (core.act, core.dve)[b % 2]
        e.wait(t)
        copy = e.eng.tensor_copy if b % 2 else e.eng.copy
        w = len(tiles) * P
        t = core.ev["bank read", bank] = e.done(copy(dst[:, b, 0:w], core.bank[bank][:, 0:w]))
    return t


def staged(core, units):
    depth = max(len(u) for u in units)
    for step in range(len(units) + depth - 1):
        for s in reversed(range(depth)):
            n = step - s
            if 0 <= n < len(units) and s < len(units[n]):
                units[n][s]()


def soft_buffers(core, st):
    core.E = [sb(core, f"exp{b}", [P, T], stack=st) for b in range(3)]
    core.ET = [sb(core, f"expT{b}", [P, T], stack=st) for b in range(2)]
    core.qs = [sb(core, f"q_pair{s}", [P, T], stack=st) for s in range(2)]
    core.ks = [sb(core, f"k_pair{s}", [P, T], stack=st) for s in range(2)]
    core.on = [sb(core, f"o_tokens{s}", [P, NB, P], stack=st) for s in range(2)]


def softmax(core, n, b, logits, mask, ready):
    e, lb = core.E[n % 3], n % 3
    note = {}
    neg, total = core.small[:, 2 * n:2 * n + 1], core.small[:, 2 * n + 1:2 * n + 2]

    def first():
        core.pe.wait(core.ev["bank read", lb], core.ev[ready])
        w = P * (b + 1)
        note["logits"] = core.pe.done(logits(core.bank[lb][:, 0:w], b))

    def second():
        w = P * (b + 1)
        core.dve.wait(note["logits"], core.ev["exp turned", n % 3])
        t = core.ev["bank read", lb] = core.dve.done(core.dve.eng.tensor_tensor_reduce(
            e[:, 0:w], core.bank[lb][:, 0:w], mask(b), -1.0, 3.0e38, ALU.add, ALU.min, neg))
        core.act.wait(t)
        note["exp"] = core.act.done(core.act.eng.activation(
            e[:, 0:w], e[:, 0:w], ACT.Exp, bias=neg, scale=-1.0, accum_out=total))
    note["e"], note["total"] = e, total
    return [first, second], note


def times_values(core, n, b, note, key, values, width, out, finish):
    tb, ob = 3 + n % 2, 5 + n % 2
    eT = core.ET[n % 2]

    def third():
        w = P * (b + 1)
        core.pe.wait(note[key], core.ev["bank read", tb])
        for j in range(b + 1):
            ins = core.pe.eng.transpose(core.bank[tb][:, j * P:(j + 1) * P], note["e"][:, j * P:(j + 1) * P], const(core, "ident"))
        t = core.pe.done(ins)
        core.ev["exp turned", note.get("slot", n % 3)] = t
        en = (core.act, core.dve)[n % 2]
        en.wait(t, core.ev["expT used", n % 2])
        copy = en.eng.tensor_copy if n % 2 else en.eng.copy
        note["eT"] = core.ev["bank read", tb] = en.done(copy(eT[:, 0:w], core.bank[tb][:, 0:w]))

    def fourth():
        core.pe.wait(note["eT"], core.ev["bank read", ob])
        for j in range(b + 1):
            ins = core.pe.eng.matmul(core.bank[ob][:, 0:width], eT[:, j * P:(j + 1) * P], values(j),
                                     start=j == 0, stop=j == b)
        t = core.ev["expT used", n % 2] = core.pe.done(ins)
        finish(core.bank[ob][:, 0:width], t, ob)
    return [third, fourth]


def normalised(core, n, dst, note):
    inv = core.small[:, 128 + n:129 + n]

    def finish(product, tick, ob):
        core.dve.wait(note["exp"])
        t = core.dve.done(core.dve.eng.reciprocal(inv, note["total"]))
        core.dve.wait(t, tick)
        core.ev["heads written"] = core.ev["bank read", ob] = core.dve.done(core.dve.eng.tensor_scalar(dst, product, inv, None, ALU.mult))
    return finish


def store_heads(core, s, m, bank=7):
    core.pe.wait(core.ev["bank read", bank], core.ev["heads written"])
    for b in range(NB):
        ins = core.pe.eng.transpose(core.bank[bank][:, b * P:(b + 1) * P], core.on[s][:, b, :], const(core, "ident"))
    t = core.pe.done(ins)
    core.act.wait(t)
    core.ev["bank read", bank] = core.act.done(core.act.eng.copy(
        core.u[:, bass.ds(m, 1), :].rearrange("p o t -> p (o t)"), core.bank[bank]))


def causal(core, b):
    return const(core, "causal")[:, T - P * (b + 1):T]


def pair_products(core, s, a, k=None):
    q, k = core.qs[s], core.ks[s] if k is None else k
    r = slice(a * HD, (a + 1) * HD)

    def logits(out, b):
        return core.pe.eng.matmul(out, q[r, b * P:(b + 1) * P], k[r, 0:P * (b + 1)], start=True, stop=True)
    return logits


def layer_ab(core):
    nc, pe, act, dve = core.nc, core.pe, core.act, core.dve
    norm(core, "g_a0", core.u)
    with ExitStack() as st:
        y = sb(core, "y_ab", [P, N_AB, T], stack=st)
        AQ, AQI, BQ, BK, CKV, MI, MF, BV = 0, 4, 8, 12, 16, 18, 19, 20
        project(core, CH_AB, N_AB, y)
        for e in (pe, act, dve, core.pool):
            e.eng.wait_ge(core.tables, 16)
        soft_buffers(core, st)
        wuk = landing(core, "w_uk", [P, 2, T], st)
        wuv = landing(core, "w_uv", [P, 2, T], st)
        wuk.load(core.sp, core.t["w_uk"])
        wuv.load(core.sp, core.t["w_uv"])
        vb = sb(core, "v_fox", [P, NB, T], stack=st)
        vd = sb(core, "v_dsa", [P, NB, T], stack=st)
        kd = sb(core, "k_dsa", [P, NB, T], stack=st)
        add = sb(core, "dsa_mask", [P, 3, T], stack=st)
        ki = y[:, BV, :]
        tok = core.on[0]
        to_tokens(core, vb, [y[:, BV + m, :] for m in range(4)])
        tok_t = to_tokens(core, tok, [y[:, MF, :]])
        ck = [y[:, CKV + r, :] for r in range(2)]
        t = sum_squares(core, ck, const(core, "ones"), 7)
        core.ev["bank read", 7], t = inverse_root(core, core.rs, core.bank[7], 256, t)
        dve.wait(t)
        for r in range(2):
            ckt = dve.done(dve.eng.scalar_tensor_tensor(ck[r], ck[r], vec(core, "g_kv")[:, r:r + 1], core.rs, ALU.mult, ALU.mult))
        mi = y[:, MI, :]
        act.wait(ckt)
        t = sum_squares(core, [mi], const(core, "pair_ones"), 6, after=(ckt,))
        core.ev["bank read", 6], t = inverse_root(core, core.rs[0:HD], core.bank[6][0:HD], HD, t)
        dve.wait(t)
        t = dve.done(dve.eng.scalar_tensor_tensor(mi[0:HD], mi[0:HD], vec(core, "g_ki")[0:HD], core.rs[0:HD], ALU.mult, ALU.mult))
        dve.wait(t)
        t = rope(core, mi, mi, "rope_c", "rope_s", 5, core.sq, (t,))
        pe.wait(t, core.ev["bank read", 4])
        t = pe.done(pe.eng.matmul(core.bank[4], const(core, "dup"), mi, start=True, stop=True))
        act.wait(t)
        core.ev["bank read", 4] = act.done(act.eng.copy(ki, core.bank[4]))
        wuk.wait(pe)
        wuv.wait(pe)
        pe.wait(ckt)
        for m in range(4):
            pe.wait(core.ev["bank read", m])
            for r in range(2):
                pe.eng.matmul(core.bank[m], wuk.ap[:, r, m * P:(m + 1) * P], ck[r], start=r == 0, stop=False)
            t = pe.done(pe.eng.matmul(core.bank[m], const(core, "sel_rope"), mi, start=False, stop=True))
            evacuate(core, m, kd[:, m, :], t, m)
        z, a, s = core.ks[0][0:8], core.ks[1][0:8], core.on[1][0:8].rearrange("p b d -> p (b d)")
        t = dve.done(dve.eng.tensor_scalar(z, y[0:8, MF, :], vec(core, "b_f")[0:8], None, ALU.add))
        dve.wait(t)
        t = dve.done(dve.eng.scalar_tensor_tensor(a, z, -1.0, z, ALU.mult, ALU.min))
        act.wait(t)
        t = act.done(act.eng.activation(a, a, ACT.Exp))
        act.wait(t)
        t = act.done(act.eng.activation(a, a, ACT.Ln, bias=1.0))
        dve.wait(t)
        t = dve.done(dve.eng.scalar_tensor_tensor(a, z, 0.0, a, ALU.min, ALU.subtract))
        dve.wait(t)
        t = dve.done(dve.eng.tensor_tensor_scan(s, const(core, "ones")[0:8, 0:1].to_broadcast([8, T]), a, 0.0, ALU.mult, ALU.add))
        dve.wait(t)
        ct = dve.done(dve.eng.tensor_scalar(a, s, -1.0, None, ALU.mult))
        for b in range(NB):
            pe.wait(core.ev["bank read", b])
            for r in range(2):
                ins = pe.eng.matmul(core.bank[b], ck[r][:, b * P:(b + 1) * P], wuv.ap[:, r, :], start=r == 0, stop=r == 1)
            t = pe.done(ins)
            evacuate(core, b, vd[:, b, :], t, b)
        cum, cum_l = y[:, CKV:CKV + 4, :], Landing(None, sem(core, "landed_cum"))
        core.sp.wait(ct, t)
        for h in range(8):
            for r, src in ((0, a), (32, s)):
                row = HD * (h % 2) + r
                core.sp.eng.dma_start(cum[row:row + 1, h // 2, :], src[h:h + 1]).then_inc(cum_l.sem, 16)
        fls, frs = (y[:, BV + 1, :], y[:, BV + 2, :]), (y[:, BV + 3, :], core.rs)
        for zero in fls + frs:
            dve.done(dve.eng.memset(zero, 0.0))
        dve.wait((dve.sem, dve.n))
        for h in range(2):
            for a in range(2):
                dve.done(dve.eng.memset(fls[h][HD * a:HD * a + 1], 1.0))
                dve.done(dve.eng.memset(frs[h][HD * a + 32:HD * a + 33], 1.0))
        dve.wait(tok_t)
        wsc = sb(core, "w_idx", [P, NB, 8], stack=st)
        dve.done(dve.eng.tensor_scalar(wsc, tok[:, :, 32:40], 8 ** -0.5 * HD ** -0.5, None, ALU.mult))
        dve.done(dve.eng.memset(add, 0.0))
        with loop(core, 2) as i:
            n = 0
            rel_free = [None] * 3
            added = [None] * NB
            for h in range(2):
                m = i * 2 + h
                qt = rope(core, core.qs[h], tile(y, m + AQI), "rope_c", "rope_s", 6 + h, core.sq)
                for b in (1, 2, 3):
                    w = P * (b + 1)
                    for a in range(2):
                        pe.wait(qt, core.ev["bank read", n % 3])
                        t = pe.done(pair_products(core, h, a, k=ki)(core.bank[n % 3][:, 0:w], b))
                        act.wait(t, rel_free[n % 3])
                        t = core.ev["bank read", n % 3] = act.done(act.eng.activation(core.E[n % 3][:, 0:w], core.bank[n % 3][:, 0:w], ACT.Relu))
                        dve.wait(added[b])
                        dve.wait(t)
                        t = rel_free[n % 3] = added[b] = dve.done(dve.eng.scalar_tensor_tensor(
                            add[:, b - 1, 0:w], core.E[n % 3][:, 0:w], wsc[:, b, bass.ds(m * 2 + a, 1)],
                            add[:, b - 1, 0:w], ALU.mult, ALU.add))
                        n += 1
            barrier(core)
        dve.eng.wait_ge(cum_l.sem, 16 * 16)
        for b in (1, 2, 3):
            s = add[:, b - 1, 0:P * (b + 1)]
            dve.done(dve.eng.tensor_tensor(s, s, causal(core, b), ALU.add))

        def top_step(b, replace):
            def step():
                s, top = add[:, b - 1, 0:P * (b + 1)], core.small[:, 200 + 8 * b:208 + 8 * b]
                dve.wait(core.ev["top", b])
                ins = dve.eng.match_replace(s, top, s, TAKEN) if replace else dve.eng.max(top, s)
                core.ev["top", b] = dve.done(ins)
            return step
        top_steps = [top_step(b, replace) for r in range(TOPK // 8 // 2) for replace in (False, True) for b in (1, 2, 3)]
        with loop(core, 2) as i:
            def fox_pair(h):
                dve.done(dve.eng.tensor_copy(core.ks[h], tile(y, i * 2 + (h + BK))))
                t = dve.done(dve.eng.tensor_scalar(core.qs[h], tile(y, i * 2 + (h + BQ)), SCALE, None, ALU.mult))
                for a in range(2):
                    for row, dst in ((HD * a, frs[h]), (HD * a + 32, fls[h])):
                        t = dve.done(dve.eng.tensor_copy(dst[row:row + 1], tile(cum[row:row + 1], i * 2 + h)))
                core.ev["q ready", h] = t

            def products(h, a):
                def logits(out, b):
                    r = slice(a * HD, (a + 1) * HD)
                    pe.eng.matmul(out, core.qs[h][r, b * P:(b + 1) * P], core.ks[h][r, 0:P * (b + 1)], start=True, stop=False)
                    return pe.eng.matmul(out, fls[h][r, b * P:(b + 1) * P], frs[h][r, 0:P * (b + 1)], start=False, stop=True)
                return logits
            two_pairs(core, i, fox_pair, products, lambda b: causal(core, b), vb, 4, top_steps)
            barrier(core)
        for b in (1, 2, 3):
            s = add[:, b - 1, 0:P * (b + 1)]
            dve.done(dve.eng.tensor_scalar(s, s, TAKEN / 2, NEG, ALU.is_gt, ALU.mult))
        with loop(core, 2) as i:
            def dsa_pair(h):
                dve.done(dve.eng.tensor_copy(core.ks[h], tile(kd, i * 2 + h)))
                core.ev["q ready", h] = rope(core, core.qs[h], tile(y, i * 2 + (h + AQ)), "rope_cq", "rope_sq", 7, core.sq)
            mask = lambda b: causal(core, 0) if b == 0 else add[:, b - 1, 0:P * (b + 1)]
            two_pairs(core, i, dsa_pair, lambda h, a: pair_products(core, h, a), mask, vd, 0)
            barrier(core)
    add_projection(core, CH_ABO)


def two_pairs(core, i, prepare, products, mask, values, out, beside=()):
    units, n = [], 0
    prepare(0)
    for h in range(2):
        for b in range(NB):
            for a in range(2):
                s, note = softmax(core, n, b, products(h, a), mask, ("q ready", h))
                dst = core.on[h][:, b, a * HD:(a + 1) * HD]
                val = lambda j, h=h, a=a: values[:, j, bass.ds(i * 2 * P + (h * P + a * HD), HD)]
                units.append(s + times_values(core, n, b, note, "exp", val, HD, None, normalised(core, n, dst, note)))
                n += 1
            if h == 0 and b == 1:
                units.append([lambda: prepare(1)])
        units[-1].append(lambda h=h: store_heads(core, h, i * 2 + (h + out)))
    beside = iter(beside)

    def followed(stage):
        def both():
            stage()
            step = next(beside, None)
            if step is not None:
                step()
        return both
    units = [[followed(stage) for stage in u[:3]] + u[3:] for u in units]
    staged(core, units)
    for step in beside:
        step()




def layer_c(core):
    pe, act, dve = core.pe, core.act, core.dve
    norm(core, "g_a1", core.u, summed=True)
    with ExitStack() as st:
        y = sb(core, "y_c", [P, N_C, T], stack=st)
        KC, KS, KW, VC, VS, VW, GL = 8, 9, 10, 11, 12, 13, 14
        project(core, CH_C, N_C, y)
        soft_buffers(core, st)
        w1 = {n: landing(core, f"cmp_{n}1", [P, CMP_LEN, P], st) for n in "kv"}
        k2 = landing(core, "cmp_k2", [P, 2, P], st)
        v2 = landing(core, "cmp_v2", [P, HD], st)
        for n in "kv":
            w1[n].load(core.sp, core.t[f"cmp_{n}1"])
        k2.load(core.sp, core.t["cmp_k2"])
        v2.load(core.sp, core.t["cmp_v2"])
        vs = sb(core, "v_sel", [P, NB, P], stack=st)
        vw = sb(core, "v_win", [P, NB, P], stack=st)
        gt = sb(core, "gates", [P, NB, P], stack=st)
        to_tokens(core, vs, [y[:, VS, :]])
        to_tokens(core, vw, [y[:, VW, :]])
        t = to_tokens(core, gt, [y[:, GL, :]])
        g = gt[:, :, 0:48]
        dve.wait(t)
        dve.wait(core.ev["bank read", 0], core.ev["bank read", 1], core.ev["bank read", 2], core.ev["bank read", 3])
        t = dve.done(dve.eng.tensor_tensor(g, g, vec(core, "b_gate").unsqueeze(1).to_broadcast([P, NB, 48]), ALU.add))
        act.wait(t)
        t = act.done(act.eng.activation(g, g, ACT.Exp, scale=-1.0))
        dve.wait(t)
        t = dve.done(dve.eng.tensor_scalar(g, g, 1.0, None, ALU.add))
        dve.wait(t)
        dve.done(dve.eng.reciprocal(g, g))
        t = None
        for j in (KC, KS, KW):
            t = rope(core, y[:, j, :], y[:, j, :], "rope_c", "rope_s", 4 + j % 2, core.sq, (t,))
            dve.wait(t)
        xg = {"k": sb(core, "win_k", [P, CMP_LEN, 2, 32], stack=st),
              "v": y[:, VS:VS + 4, :].rearrange("p o t -> p (o t)").rearrange("p (l a n) -> p l a n", a=2, n=32)}
        ready = {}
        for n, j in (("k", KC), ("v", VC)):
            wins = y[:, j, :].rearrange("p (n l) -> p l n", l=CMP_STRIDE)
            for a in range(2):
                r = slice(a * HD, (a + 1) * HD)
                dve.done(dve.eng.memset(xg[n][r, :, 1 - a, :], 0.0))
                dve.done(dve.eng.tensor_copy(xg[n][r, 0:16, a, 0:N_CMP], wins[r, :, 0:N_CMP]))
                dve.done(dve.eng.tensor_copy(xg[n][r, 16:32, a, 0:N_CMP], wins[r, :, 1:N_CMP + 1]))
                ready[n] = dve.done(dve.eng.tensor_copy(xg[n][r, :, a, N_CMP:32], vec(core, "pe_" + n)[r].unsqueeze(2)))
        hid = sb(core, "hid", [P, 4, 32], stack=st)
        hz = sb(core, "hid_z", [P, 4, 32], stack=st)
        for x, n in enumerate("kv"):
            w1[n].wait(pe)
            pe.wait(ready[n], core.ev["bank read", x])
            for l in range(CMP_LEN):
                ins = pe.eng.matmul(core.bank[x][:, 0:64], w1[n].ap[:, l, :], xg[n][:, l, :, :].rearrange("p a n -> p (a n)"),
                                    start=l == 0, stop=l == CMP_LEN - 1)
            t = pe.done(ins)
            dve.wait(t)
            t = core.ev["bank read", x] = dve.done(dve.eng.tensor_copy(
                hid[:, 2 * x:2 * x + 2, :].rearrange("p a n -> p (a n)"), core.bank[x][:, 0:64]))
        dve.wait(t)
        seq = []
        two_c = 2.0 * float(np.sqrt(2.0 / np.pi))
        t = dve.done(dve.eng.tensor_tensor(hid[:, :, 0:N_CMP], hid[:, :, 0:N_CMP],
                                           hid[:, :, N_CMP:32].to_broadcast([P, 4, N_CMP]), ALU.add))
        dve.wait(t)
        t = dve.done(dve.eng.tensor_tensor(hz, hid, hid, ALU.mult))
        dve.wait(t)
        t = dve.done(dve.eng.tensor_scalar(hz, hz, 0.044715, 1.0, ALU.mult, ALU.add))
        dve.wait(t)
        t = dve.done(dve.eng.tensor_tensor(hz, hz, hid, ALU.mult))
        act.wait(t)
        t = act.done(act.eng.activation(hz, hz, ACT.Exp, scale=-two_c))
        dve.wait(t)
        t = dve.done(dve.eng.tensor_scalar(hz, hz, 1.0, None, ALU.add))
        dve.wait(t)
        t = dve.done(dve.eng.reciprocal(hz, hz))
        dve.wait(t)
        t = dve.done(dve.eng.tensor_tensor(hid, hid, hz, ALU.mult))
        dve.wait(t)
        kc = sb(core, "k_cmp", [P, 32], stack=st)
        rep = sb(core, "hid_rep", [P, 4, 32], stack=st)
        vcd = sb(core, "v_cmp", [P, 4, HD], stack=st)
        dve.done(dve.eng.tensor_copy(rep[:, 0:2], hid[:, 2:4]))
        tr = dve.done(dve.eng.tensor_copy(rep[:, 2:4], hid[:, 2:4]))
        t2 = dve.done(dve.eng.memset(vcd, 0.0))
        k2.wait(pe)
        v2.wait(pe)
        pe.wait(t, tr, core.ev["bank read", 0], core.ev["bank read", 1])
        for a in range(2):
            ins = pe.eng.matmul(core.bank[0][:, 0:32], k2.ap[:, a, :], hid[:, a, :], start=a == 0, stop=a == 1)
        t = pe.done(ins)
        dve.wait(t)
        core.ev["bank read", 0] = dve.done(dve.eng.tensor_copy(kc, core.bank[0][:, 0:32]))
        t = pe.done(pe.eng.matmul(core.bank[1][:, 0:HD], rep.rearrange("p a n -> p (a n)"), v2.ap, start=True, stop=True))
        dve.wait(t, t2)
        for r in range(4):
            t = dve.done(dve.eng.tensor_copy(vcd[32 * r:32 * r + 32, r, :], core.bank[1][32 * r:32 * r + 32, 0:HD]))
        core.ev["bank read", 1] = t
        pc = sb(core, "p_cmp", [P, 8, 32], stack=st)
        pcT = sb(core, "p_cmpT", [P, 2, P], stack=st)
        oc = sb(core, "o_cmp", [P, NB, P], stack=st)
        gs = [sb(core, f"gate_pair{h}", [P, NB, 6], stack=st) for h in range(2)]
        dve.wait(t)
        with loop(core, 4) as i:
            def prepare(h):
                core.ev["gates", h] = dve.done(dve.eng.tensor_copy(gs[h], gt[:, :, bass.ds(i * 12 + 6 * h, 6)]))
                core.ev["q ready", h] = rope(core, core.qs[h], tile(y, i * 2 + h), "rope_cq", "rope_sq", 7, core.sq)

            units, n = [], 0
            prepare(0)
            for h in range(2):
                units.append(compressed(core, h, kc, vcd, gs[h], pc, pcT, oc))
                for b in range(NB):
                    for x, (kk, vv) in enumerate(((KS, vs), (KW, vw))):
                        for a in range(2):
                            s, note = softmax(core, n, b, pair_products(core, h, a, k=y[:, kk, :]), lambda b: causal(core, b), ("q ready", h))
                            dst = core.on[h][:, b, a * HD:(a + 1) * HD]
                            val = lambda j, a=a, vv=vv: vv[:, j, a * HD:(a + 1) * HD]
                            fin = gated(core, n, dst, note, gs[h][:, b, 3 * a + 1 + x:3 * a + 2 + x], (h, b, a), x == 0)
                            units.append(s + times_values(core, n, b, note, "exp", val, HD, None, fin))
                            n += 1
                    if h == 0 and b == 2:
                        units.append([lambda: prepare(1)])

                def finish(h=h):
                    dve.wait(core.ev["heads written"], core.ev["o_cmp", h])
                    core.ev["heads written"] = core.ev["o_cmp added"] = dve.done(dve.eng.tensor_tensor(core.on[h], core.on[h], oc, ALU.add))
                units[-1].append(finish)
                units[-1].append(lambda h=h: store_heads(core, h, i * 2 + h))
            staged(core, units)
            barrier(core)
    add_projection(core, CH_CO)


def compressed(core, s, kc, vcd, gates, pc, pcT, oc):
    pe, act, dve = core.pe, core.act, core.dve
    mx, sm = core.small[:, 300 + 20 * s:308 + 20 * s], core.small[:, 310 + 20 * s:318 + 20 * s]
    flat = pc.rearrange("p a n -> p (a n)")
    bc = lambda v: v.unsqueeze(2).to_broadcast([P, 8, 32])
    by_head = lambda v: v.rearrange("p (b a) -> p b a", a=2)
    at = {}

    def logits():
        pe.wait(core.ev["q ready", s], core.ev["bank read", 7])
        for a in range(2):
            r = slice(a * HD, (a + 1) * HD)
            if a:
                pe.wait(at["logits"])
            for b in range(NB):
                ins = pe.eng.matmul(core.bank[7][:, a * P + b * 32:a * P + (b + 1) * 32],
                                    core.qs[s][r, b * P:(b + 1) * P], kc[r, :], start=True, stop=True)
            at["logits"] = pe.done(ins)

    def exps():
        dve.wait(at["logits"], core.ev["p_cmp turned"])
        for a in range(2):
            t = core.ev["bank read", 7] = dve.done(dve.eng.tensor_tensor(
                pc[:, a::2, :], core.bank[7][:, a * P:(a + 1) * P].rearrange("p (b n) -> p b n", n=32),
                const(core, "cmp_add").rearrange("p (b a n) -> p b a n", a=2, n=32)[:, :, a, :], ALU.add))
        dve.wait(t)
        t = dve.done(dve.eng.tensor_reduce(mx, pc, AX.X, ALU.max))
        dve.wait(t)
        t = dve.done(dve.eng.tensor_tensor(pc, pc, bc(mx), ALU.subtract))
        act.wait(t)
        at["exp"] = act.done(act.eng.activation(pc, pc, ACT.Exp))

    def weights():
        dve.wait(at["exp"])
        t = dve.done(dve.eng.tensor_tensor(flat, flat, const(core, "cmp_one"), ALU.mult))
        dve.wait(t)
        t = dve.done(dve.eng.tensor_reduce(sm, pc, AX.X, ALU.add))
        dve.wait(t)
        t = dve.done(dve.eng.tensor_scalar(sm, sm, 1e-30, None, ALU.max))
        dve.wait(t)
        t = dve.done(dve.eng.reciprocal(sm, sm))
        dve.wait(t, core.ev["gates", s])
        t = dve.done(dve.eng.tensor_tensor(by_head(sm), by_head(sm), gates[:, :, 0:4:3], ALU.mult))
        dve.wait(t)
        at["weights"] = dve.done(dve.eng.tensor_tensor(pc, pc, bc(sm), ALU.mult))

    def turned():
        pe.wait(at["weights"], core.ev["bank read", 7])
        for h in range(2):
            ins = pe.eng.transpose(core.bank[7][:, h * P:(h + 1) * P], flat[:, h * P:(h + 1) * P], const(core, "ident"))
        t = core.ev["p_cmp turned"] = pe.done(ins)
        act.wait(t, core.ev["p_cmpT used"])
        at["pcT"] = core.ev["bank read", 7] = act.done(act.eng.copy(pcT.rearrange("p h q -> p (h q)"), core.bank[7][:, 0:256]))

    def product():
        pe.wait(at["pcT"], core.ev["bank read", 7])
        for h in range(2):
            ins = pe.eng.matmul(core.bank[7][:, h * 256:(h + 1) * 256], pcT[:, h, :], vcd.rearrange("p r d -> p (r d)"),
                                start=True, stop=True)
        t = core.ev["p_cmpT used"] = pe.done(ins)
        act.wait(t, core.ev["o_cmp added"])
        core.ev["bank read", 7] = core.ev["o_cmp", s] = act.done(act.eng.copy(oc.rearrange("p b d -> p (b d)"), core.bank[7]))
    return [logits, exps, weights, turned, product]


def gated(core, n, dst, note, gate, key, first):
    inv = core.small[:, 128 + n:129 + n]

    def finish(product, tick, ob):
        core.dve.wait(note["exp"])
        t = core.dve.done(core.dve.eng.reciprocal(inv, note["total"]))
        core.dve.wait(t, core.ev["gates", key[0]])
        t = core.dve.done(core.dve.eng.tensor_tensor(inv, inv, gate, ALU.mult))
        core.dve.wait(t, tick, core.ev["gated", key])
        if first:
            ins = core.dve.eng.tensor_scalar(dst, product, inv, None, ALU.mult)
        else:
            ins = core.dve.eng.scalar_tensor_tensor(dst, product, inv, dst, ALU.mult, ALU.add)
        core.ev["heads written"] = core.ev["bank read", ob] = core.ev["gated", key] = core.dve.done(ins)
    return finish


def layer_2(core):
    pe, act, dve = core.pe, core.act, core.dve
    norm(core, "g_a2", core.u)
    with ExitStack() as st:
        y = sb(core, "y_2", [P, N_2, T], stack=st)
        DQ, DK, DV, SQ, SK, SV = 0, 4, 8, 12, 16, 20
        project(core, CH_2, N_2, y)
        soft_buffers(core, st)
        vd = sb(core, "v_da", [P, NB, T], stack=st)
        vb = sb(core, "v_sb", [P, NB, T], stack=st)
        to_tokens(core, vd, [y[:, DV + m, :] for m in range(4)])
        to_tokens(core, vb, [y[:, SV + m, :] for m in range(4)])
        bf = landing(core, "bias", [P, 4, T], st)
        row = sb(core, "bias_row", [P, LV], stack=st)
        scr_sem = sem(core, "bias_out")
        scr = core.nc.dram_tensor("bias_scratch", [4, P * LV], F32, kind="Internal").ap()
        for h in range(4):
            for q in range(2):
                w = T if q == 0 else LV - T
                pe.wait(core.ev["bank read", 4 + q])
                t = pe.done(pe.eng.matmul(core.bank[4 + q][:, 0:w], vec(core, "rel")[0:BUCKETS, h * P:(h + 1) * P],
                                          const(core, "buckets")[0:BUCKETS, q * T:q * T + w], start=True, stop=True))
                act.wait(t)
                if h and q == 0:
                    act.eng.wait_ge(scr_sem, 16 * h)
                t = core.ev["bank read", 4 + q] = act.done(act.eng.copy(row[:, q * T:q * T + w], core.bank[4 + q][:, 0:w]))
            core.sp.wait(t)
            core.sp.eng.dma_start(scr[h].rearrange("(p c) -> p c", c=LV), row).then_inc(scr_sem, 16)
        core.sp.eng.wait_ge(scr_sem, 64)
        for h in range(4):
            src = scr[h, P - 1:P - 1 + P * (LV - 1)].rearrange("(p c) -> p c", c=LV - 1)[:, 0:T]
            core.sp.eng.dma_start(bf.ap[:, h, :], src).then_inc(bf.sem, 16)
        lam = core.small[:, 400:404]
        lt = core.E[0][:, 0:P]
        lv = vec(core, "lam").rearrange("p (s x) -> p s x", s=2)
        t = dve.done(dve.eng.tensor_tensor(lt, lv[:, 0, :], lv[:, 1, :], ALU.mult))
        dve.wait(t)
        t = dve.done(dve.eng.tensor_reduce(lam[:, 0:2], lt.rearrange("p (s x) -> p s x", s=2), AX.X, ALU.add))
        act.wait(t)
        t = act.done(act.eng.activation(lam[:, 0:2], lam[:, 0:2], ACT.Exp))
        dve.wait(t)
        t = dve.done(dve.eng.tensor_tensor(lam[:, 2:3], lam[:, 0:1], lam[:, 1:2], ALU.subtract))
        dve.wait(t)
        t = dve.done(dve.eng.tensor_scalar(lam[:, 3:4], lam[:, 2:3], LAMBDA_INIT, None, ALU.add))
        sg = sb(core, "subln_s", [P, 1], stack=st)
        gq = sb(core, "gq_s", [P, 1], stack=st)
        dve.done(dve.eng.tensor_scalar(sg, vec(core, "subln"), 1.0 - LAMBDA_INIT, None, ALU.mult))
        dve.wait(dve.done(dve.eng.tensor_scalar(gq, vec(core, "g_qn"), SCALE, None, ALU.mult)))
        norm_tiles(core, [tile(y, DQ + m) for m in range(4)] + [tile(y, DK + m) for m in range(4)],
                   [tile(y, DV + m) for m in range(4)] + [tile(y, SV + m) for m in range(4)],
                   [("pair_ones", HD, gq)] * 4 + [("pair_ones", HD, vec(core, "g_kn"))] * 4)
        dve.eng.wait_ge(bf.sem, 64)
        t = dve.done(dve.eng.tensor_tensor(bf.ap, bf.ap, const(core, "chunked").unsqueeze(1).to_broadcast([P, 4, T]), ALU.add))
        bm = [sb(core, f"bias_head{h}", [P, T], stack=st) for h in range(2)]
        with loop(core, 2) as i:
            def prepare(h):
                dve.done(dve.eng.tensor_copy(bm[h], tile(bf.ap, i * 2 + h)))
                dve.done(dve.eng.tensor_copy(core.qs[h], tile(y, i * 2 + (h + DQ))))
                core.ev["q ready", h] = dve.done(dve.eng.tensor_copy(core.ks[h], tile(y, i * 2 + (h + DK))))
            prepare(0)
            units = []
            for h in range(2):
                for b in range(NB):
                    n0, n1, v = 8 * h + 2 * b, 8 * h + 2 * b + 1, NB * h + b
                    mask = lambda b, h=h: bm[h][:, T - P * (b + 1):T]
                    s0, note0 = softmax(core, n0, b, pair_products(core, h, 0), mask, ("q ready", h))
                    s1, note1 = softmax(core, n1, b, pair_products(core, h, 1), mask, ("q ready", h))
                    units.append(s0)
                    units.append(s1 + [difference(core, v, b, n0, n1, note0, note1, lam)]
                                 + times_values(core, v, b, note0, "diff",
                                                lambda j, h=h: vd[:, j, bass.ds(i * 2 * P + h * P, P)], P, None,
                                                plain(core, core.on[h][:, b, :])))
                    if h == 0 and b == 2:
                        units.append([lambda: prepare(1)])
                units[-1].append(lambda h=h: store_heads(core, h, i * 2 + h))
            staged(core, units)
            barrier(core)
        zs = [[y[:, 4 * a + j, :] for j in range(NB)] for a in range(2)]
        sps = [[y[:, (DV, SV)[a] + j, :] for j in range(NB)] for a in range(2)]
        parts = [(a, j, T - P * j) for a in range(2) for j in range(NB - 1, -1, -1)]
        with loop(core, 4) as m:
            dve.done(dve.eng.tensor_copy(core.ks[0], tile(y, m + SK)))
            qt = dve.done(dve.eng.tensor_scalar(core.qs[0], tile(y, m + SQ), SCALE, None, ALU.mult))
            lt, zt, spt, at = {}, {}, {}, {}
            for a, j, w in parts:
                bank, z, s, r = 4 * a + j, zs[a][j], sps[a][j][:, 0:w], slice(a * HD, (a + 1) * HD)
                pe.wait(qt)
                t = pe.done(pe.eng.matmul(core.bank[bank][:, 0:w], core.ks[0][r, j * P:(j + 1) * P], core.qs[0][r, j * P:T], start=True, stop=True))
                dve.wait(t)
                t = dve.done(dve.eng.tensor_tensor(z[:, 0:P], core.bank[bank][:, 0:P], const(core, "strict"), ALU.add))
                if w > P:
                    t = dve.done(dve.eng.tensor_copy(z[:, P:w], core.bank[bank][:, P:w]))
                zt[a, j] = t
                dve.wait(t)
                t = dve.done(dve.eng.scalar_tensor_tensor(s, z[:, 0:w], -1.0, z[:, 0:w], ALU.mult, ALU.min))
                act.wait(t)
                lt[a, j] = act.done(act.eng.activation(s, s, ACT.Exp))
            for a, j, w in parts:
                s = sps[a][j][:, 0:w]
                act.wait(lt[a, j])
                t = act.done(act.eng.activation(s, s, ACT.Ln, bias=1.0))
                dve.wait(t)
                spt[a, j] = dve.done(dve.eng.scalar_tensor_tensor(s, zs[a][j][:, 0:w], 0.0, s, ALU.max, ALU.add))
            for a, j, w in parts:
                bank, z = 4 * a + j, zs[a][j][:, 0:w]
                pe.wait(zt[a, j])
                pe.wait(spt[a, j])
                ins = pe.eng.matmul(core.bank[bank][:, 0:w], const(core, "tri_from"), sps[a][j][:, 0:w], start=True, stop=j == 3)
                for jj in range(j + 1, 4):
                    ins = pe.eng.matmul(core.bank[bank][:, P * (jj - j):w], const(core, "ones"), sps[a][jj][:, 0:T - P * jj],
                                        start=False, stop=jj == 3)
                dve.wait(pe.done(ins))
                t = core.ev["bank read", bank] = dve.done(dve.eng.tensor_tensor(z, z, core.bank[bank][:, 0:w], ALU.subtract))
                act.wait(t)
                at[a, j] = act.done(act.eng.activation(z, z, ACT.Exp))
            for a in range(2):
                bank = 4 * a + 3
                pe.wait(core.ev["bank read", bank], at[a, 0])
                for b in range(NB):
                    for j in range(b + 1):
                        ins = pe.eng.matmul(core.bank[bank][:, b * HD:(b + 1) * HD], zs[a][j][:, P * (b - j):P * (b - j + 1)],
                                            vb[:, j, bass.ds(m * P + a * HD, HD)], start=j == 0, stop=j == b)
                dve.wait(pe.done(ins))
                core.ev["bank read", bank] = core.ev["heads written"] = dve.done(dve.eng.tensor_copy(
                    core.on[0][:, :, a * HD:(a + 1) * HD], core.bank[bank][:, 0:NB * HD].rearrange("p (b d) -> p b d", d=HD)))
            store_heads(core, 0, m + 4)
            barrier(core)
        norm_tiles(core, [core.u[:, m, :] for m in range(KT)], [y[:, m, :] for m in range(KT)],
                   [("ones", P, sg)] * 4 + [("pair_ones", HD, vec(core, "sb_g"))] * 4)
        barrier(core)
    add_projection(core, CH_2O)


def difference(core, v, b, n0, n1, note0, note1, lam):
    def stage():
        dve, w = core.dve, P * (b + 1)
        inv = core.small[:, 128 + 2 * v:130 + 2 * v]
        dve.wait(note0["exp"], note1["exp"])
        dve.done(dve.eng.reciprocal(inv[:, 0:1], note0["total"]))
        t = dve.done(dve.eng.reciprocal(inv[:, 1:2], note1["total"]))
        dve.wait(t)
        t = dve.done(dve.eng.tensor_tensor(inv[:, 1:2], inv[:, 1:2], lam[:, 3:4], ALU.mult))
        dve.wait(t)
        t = dve.done(dve.eng.tensor_scalar(note1["e"][:, 0:w], note1["e"][:, 0:w], inv[:, 1:2], None, ALU.mult))
        dve.wait(t)
        t = dve.done(dve.eng.scalar_tensor_tensor(note0["e"][:, 0:w], note0["e"][:, 0:w], inv[:, 0:1], note1["e"][:, 0:w],
                                                  ALU.mult, ALU.subtract))
        core.ev["exp turned", n1 % 3] = t
        note0["diff"], note0["slot"] = t, n0 % 3
    return stage


def plain(core, dst):
    def finish(product, tick, ob):
        core.dve.wait(tick)
        core.ev["heads written"] = core.ev["bank read", ob] = core.dve.done(core.dve.eng.tensor_copy(dst, product))
    return finish


def norm_tiles(core, tiles, scratch, kinds):
    pe, act, dve = core.pe, core.act, core.dve
    sums, lns = [], []
    for k, src in enumerate(tiles):
        act.wait(core.ev["square summed", k % 2])
        t = act.done(act.eng.activation(core.sq[k % 2], src, ACT.Square))
        pe.wait(t, core.ev["bank read", k])
        t = core.ev["square summed", k % 2] = pe.done(pe.eng.matmul(
            core.bank[k], const(core, kinds[k][0]), core.sq[k % 2], start=True, stop=True))
        sums.append(t)
    for k, dst in enumerate(scratch):
        act.wait(sums[k])
        t = core.ev["bank read", k] = act.done(act.eng.activation(dst, core.bank[k], ACT.Ln, bias=core.eps, scale=1.0 / kinds[k][1]))
        lns.append(t)
    for k, src in enumerate(tiles):
        act.wait(lns[k])
        t = act.done(act.eng.activation(scratch[k], scratch[k], ACT.Exp, scale=-0.5))
        dve.wait(t)
        dve.done(dve.eng.scalar_tensor_tensor(src, src, kinds[k][2][:, 0:1], scratch[k], ALU.mult, ALU.mult))


def dump_x(core):
    s = sem(core, "dumped")
    core.sp.eng.dma_start(core.out, core.x).then_inc(s, 16)
    core.sp.eng.wait_ge(s, 16)


def moe(core):
    nc, pe, act, dve, pool, sp = core.nc, core.pe, core.act, core.dve, core.pool, core.sp
    core.dense.close()
    st = core.stack
    half = KT * EH // 2
    core.w = [{(n, h): landing(core, f"{n}_{q}{h}", [P, half], st) for n in ("e1", "e3", "e2") for h in range(2)}
              for q in range(2)]
    for key in core.w[0]:
        load_expert(core, 0, key, 0)
    norm(core, "g_ffn", core.u, summed=True)
    barrier(core)
    core.hscr = nc.dram_tensor("h_tokens", [T, D], F32, kind="Internal").ap()
    core.yscr = nc.dram_tensor("y_pairs", [2 * T, D], F32, kind="Internal").ap()
    core.meta = sb(core, "meta", [P, NB, NE, 4])
    core.pos = sb(core, "pos", [P, NB, NE])
    core.S = sb(core, "slot_onehot", [P, NB, P])
    core.xg = sb(core, "xg", [P, D])
    core.xT = [sb(core, f"xT{q}", [P, KT, P]) for q in range(2)]
    core.hN = sb(core, "hN", [P, EH])
    core.sig = sb(core, "sig", [P, EH])
    core.hT = sb(core, "hT", [P, EH // P, P])
    core.oN = [sb(core, f"oN{j}", [P, D]) for j in range(SETS)]
    core.mt = [sb(core, f"mt{j}", [P, 4]) for j in range(SETS)]
    core.idx = [sb(core, f"idx{j}", [P, 2], I32) for j in range(SETS)]
    core.gathered, core.scattered = sem(core, "gathered"), [sem(core, f"scattered{j}") for j in range(SETS)]
    core.idx_ready, core.o_ready = sem(core, "idx_ready"), sem(core, "o_ready")
    core.slot_out = sb(core, "slot_out", [P, 1])
    count = sb(core, "count", [P, 2], I32)
    route(core, count)
    dve.done(dve.eng.memset(core.xg, 0.0))
    barrier(core)
    dispatch(core, 0, 0, 0, 0)()
    for h in range(2):
        turn(core, 0, 0, h)
    for e in range(SETS):
        expert(core, e, e, 0, e + 1, refill=e + 2)
    barrier(core, pool=False)
    with nc.Fori(1, NE // SETS - 1) as i:
        for s in range(SETS):
            expert(core, s, i * SETS + s, i, i * SETS + (s + 1), refill=i * SETS + (s + 2))
        barrier(core, pool=False)
    for e in range(NE - SETS, NE - 1):
        expert(core, e % SETS, e, e // SETS, e + 1, refill=e + 2 if e + 2 < NE else None)
    expert(core, SETS - 1, NE - 1, NE // SETS - 1, None, prior=(core.scattered[SETS - 2], NE // SETS * 16))
    for j in range(SETS):
        pool.eng.wait_ge(core.scattered[j], NE // SETS * 16)
    barrier(core)
    most = nc.values_load(count[0:1, 0:1], min_val=0, max_val=T)
    with nc.If(most > CAP):
        with nc.Fori(0, NE) as e:
            with nc.Fori(1, T // CAP) as c:
                for key in core.w[0]:
                    load_expert(core, 0, key, e)
                extra = e * (T // CAP - 1) + (c - 1)
                rounds = extra + NE // SETS
                dispatch(core, 0, e, c, rounds)()
                for h in range(2):
                    turn(core, 0, extra + NE, h)
                expert(core, 0, extra + NE, rounds, None)
                core.pool.eng.wait_ge(core.scattered[0], rounds * 16 + 16)
                core.pool.eng.sem_inc(core.pool.sem, 1)
                core.pool.n += 1
                barrier(core)
    nc.end_ifs()
    barrier(core)
    add_choices(core)


def load_expert(core, q, key, e, *used):
    name, h = key
    w = core.t[name][e:e + 1] if isinstance(e, int) else core.t[name][bass.ds(e, 1)]
    n = core.w[q][key].ap.shape[1]
    core.w[q][key].load(core.sp, w[:, :, h * n:(h + 1) * n].rearrange("o p n -> p (o n)"), *used)


def first_of_equals(core, onehot, values, best, tmp, mr, n):
    dve = core.dve
    bc = lambda v: v.unsqueeze(2).to_broadcast([P, NB, n])
    t = dve.done(dve.eng.tensor_tensor(tmp, values, bc(best), ALU.is_equal))
    dve.wait(t)
    t = dve.done(dve.eng.tensor_tensor(tmp, tmp, const(core, "rev8")[:, 0:n].unsqueeze(1).to_broadcast([P, NB, n]), ALU.mult))
    dve.wait(t)
    t = dve.done(dve.eng.tensor_reduce(mr, tmp, AX.X, ALU.max))
    dve.wait(t)
    t = dve.done(dve.eng.tensor_tensor(onehot, tmp, bc(mr), ALU.is_equal))
    dve.wait(t)


def route(core, count):
    pe, act, dve = core.pe, core.act, core.dve
    with ExitStack() as st:
        wr = landing(core, "w_router", [P, KT, NG + NE], st)
        wr.load(core.sp, core.t["router"])
        stored = sem(core, "h_stored")
        wr.wait(pe)
        n = NG + NE
        lt = core.sig
        dve.wait(dve.done(dve.eng.memset(lt[32:64], 0.0)))
        for k in range(KT):
            ins = pe.eng.matmul(core.bank[0][0:n, :], wr.ap[:, k, :], core.u[:, k, :], start=k == 0, stop=k == KT - 1)
        dve.wait(pe.done(ins))
        t = dve.done(dve.eng.tensor_copy(lt[0:n], core.bank[0][0:n, :]))
        pe.wait(t)
        for b in range(NB):
            ins = pe.eng.transpose(core.bank[1][:, b * 64:(b + 1) * 64], lt[0:64, b * P:(b + 1) * P], const(core, "ident")[0:64, 0:64])
        t = pe.done(ins)
        lg = sb(core, "logits", [P, NB, n], stack=st)
        dve.wait(t)
        t = core.ev["bank read", 1] = dve.done(dve.eng.tensor_tensor(
            lg, core.bank[1][:, 0:NB * 64].rearrange("p (b n) -> p b n", n=64)[:, :, 0:n],
            vec(core, "b_router").unsqueeze(1).to_broadcast([P, NB, n]), ALU.add))
        dve.wait(t)
        g, e4 = lg[:, :, 0:NG], lg[:, :, NG:].rearrange("p b (g e) -> p b g e", e=EPG)
        col = lambda name: sb(core, name, [P, NB], stack=st)
        gm, gs, m1, m2, sm, mr, g1, g2 = (col(f"col{j}") for j in range(8))
        oh = sb(core, "group", [P, NB, NG], stack=st)
        eg = sb(core, "group_exp", [P, NB, NG], stack=st)
        tmp4 = sb(core, "tmp4", [P, NB, NG], stack=st)
        tmp8, pr, oh1, oh2, p2 = (sb(core, f"eight{j}", [P, NB, EPG], stack=st) for j in range(5))
        big, a1, a2, m = (sb(core, f"assign{j}", [P, NB, NG, EPG], stack=st) for j in range(4))

        def step(ins):
            dve.wait(dve.done(ins))
        step(dve.eng.tensor_reduce(gm, g, AX.X, ALU.max))
        first_of_equals(core, oh, g, gm, tmp4, mr, NG)
        bc = lambda v, k: v.unsqueeze(2).to_broadcast([P, NB, k])
        t = dve.done(dve.eng.tensor_tensor(eg, g, bc(gm, NG), ALU.subtract))
        act.wait(t)
        dve.wait(act.done(act.eng.activation(eg, eg, ACT.Exp)))
        step(dve.eng.tensor_reduce(gs, eg, AX.X, ALU.add))
        step(dve.eng.reciprocal(gs, gs))
        g8 = lambda v: v.unsqueeze(3).to_broadcast([P, NB, NG, EPG])
        e8 = lambda v: v.unsqueeze(2).to_broadcast([P, NB, NG, EPG])
        step(dve.eng.tensor_tensor(big, e4, g8(oh), ALU.mult))
        step(dve.eng.tensor_reduce(pr, big.rearrange("p b g e -> p b e g"), AX.X, ALU.add))
        step(dve.eng.tensor_reduce(m1, pr, AX.X, ALU.max))
        t = dve.done(dve.eng.tensor_tensor(pr, pr, bc(m1, EPG), ALU.subtract))
        act.wait(t)
        dve.wait(act.done(act.eng.activation(pr, pr, ACT.Exp)))
        step(dve.eng.tensor_reduce(sm, pr, AX.X, ALU.add))
        step(dve.eng.reciprocal(sm, sm))
        step(dve.eng.tensor_tensor(pr, pr, bc(sm, EPG), ALU.mult))
        step(dve.eng.tensor_reduce(m1, pr, AX.X, ALU.max))
        first_of_equals(core, oh1, pr, m1, tmp8, mr, EPG)
        step(dve.eng.scalar_tensor_tensor(p2, oh1, -2.0, pr, ALU.mult, ALU.add))
        step(dve.eng.tensor_reduce(m2, p2, AX.X, ALU.max))
        first_of_equals(core, oh2, p2, m2, tmp8, mr, EPG)
        step(dve.eng.tensor_tensor(sm, m1, m2, ALU.add))
        step(dve.eng.reciprocal(sm, sm))
        step(dve.eng.tensor_tensor(sm, sm, gs, ALU.mult))
        step(dve.eng.tensor_tensor(g1, m1, sm, ALU.mult))
        step(dve.eng.tensor_tensor(g2, m2, sm, ALU.mult))
        for a, o in ((a1, oh1), (a2, oh2)):
            step(dve.eng.tensor_copy(big, g8(oh)))
            step(dve.eng.tensor_tensor(a, big, e8(o), ALU.mult))
        step(dve.eng.tensor_tensor(m, a1, a2, ALU.add))
        flat = lambda v: v.rearrange("p b g e -> p b (g e)")
        tok = const(core, "token").unsqueeze(2).to_broadcast([P, NB, NE])
        step(dve.eng.tensor_copy(core.meta[:, :, :, 0], tok))
        step(dve.eng.scalar_tensor_tensor(flat(big), tok, 2.0, flat(a2), ALU.mult, ALU.add))
        step(dve.eng.tensor_copy(core.meta[:, :, :, 1], flat(big)))
        step(dve.eng.tensor_tensor(flat(a1), flat(a1), bc(g1, NE), ALU.mult))
        step(dve.eng.tensor_tensor(flat(a2), flat(a2), bc(g2, NE), ALU.mult))
        step(dve.eng.tensor_tensor(core.meta[:, :, :, 2], flat(a1), flat(a2), ALU.add))
        step(dve.eng.memset(core.meta[:, :, :, 3], 1.0))
        for b in range(NB):
            for h in range(2):
                bank = 4 + 2 * (b % 2) + h
                pe.wait(core.ev["bank read", bank])
                for k in range(4):
                    ins = pe.eng.transpose(core.bank[bank][:, k * P:(k + 1) * P], core.u[:, 4 * h + k, b * P:(b + 1) * P], const(core, "ident"))
                act.wait(pe.done(ins))
                t = core.ev["bank read", bank] = act.done(act.eng.copy(core.oN[b][:, h * T:(h + 1) * T], core.bank[bank]))
            core.sp.wait(t)
            core.sp.eng.dma_start(core.hscr[b * P:(b + 1) * P, :], core.oN[b]).then_inc(stored, 16)
        for key in core.w[1]:
            load_expert(core, 1, key, 1)
        mf = flat(m)
        before = core.hN[:, 0:(NB + 1) * NE].rearrange("p (b e) -> p b e", e=NE)
        dve.done(dve.eng.memset(before[:, 0, :], 0.0))
        step(dve.eng.tensor_copy(before[:, 1, :], mf[:, 0, :]))
        for b in range(1, NB):
            step(dve.eng.tensor_tensor(before[:, b + 1, :], before[:, b, :], mf[:, b, :], ALU.add))
        pe.wait((dve.sem, dve.n))
        n_b = NB * NE
        pe.eng.matmul(core.bank[1][:, 0:n_b + NE], const(core, "ones"), before.rearrange("p b e -> p (b e)"), start=True, stop=False)
        ins = pe.eng.matmul(core.bank[1][:, 0:n_b], const(core, "tri_before"), mf.rearrange("p b e -> p (b e)"), start=False, stop=True)
        dve.wait(pe.done(ins))
        step(dve.eng.tensor_tensor(core.pos, mf, core.bank[1][:, 0:NB * NE].rearrange("p (b e) -> p b e", e=NE), ALU.mult))
        step(dve.eng.tensor_tensor(core.pos, core.pos, mf, ALU.add))
        step(dve.eng.tensor_scalar(core.pos, core.pos, -1.0, None, ALU.add))
        step(dve.eng.tensor_reduce(gm[:, 0:1], core.bank[1][:, n_b:n_b + NE], AX.X, ALU.max))
        step(dve.eng.tensor_copy(count[:, 0:1], gm[:, 0:1]))
        dve.done(dve.eng.memset(core.slot_out, float(4 * T)))
        core.pool.eng.wait_ge(stored, 16 * NB)
        barrier(core)


def dispatch(core, j, e, c, rounds):
    pe, dve, pool = core.pe, core.dve, core.pool
    iota = const(core, "iota")[:, c * CAP:(c + 1) * CAP] if isinstance(c, int) else const(core, "iota")[:, bass.ds(c * CAP, CAP)]
    at = slice(e, e + 1) if isinstance(e, int) else bass.ds(e, 1)
    dve.wait(core.ev["S used"])
    for b in range(NB):
        slots = dve.done(dve.eng.tensor_scalar(core.S[:, b, :], iota, core.pos[:, b, at], None, ALU.is_equal))

    def rest():
        pe.wait(slots, core.ev["bank read", 7])
        for b in range(NB):
            ins = pe.eng.matmul(core.bank[7][:, 0:4], core.S[:, b, :], core.meta[:, b, at, :].rearrange("p o c -> p (o c)"),
                                start=b == 0, stop=b == NB - 1)
        t = core.ev["S used"] = pe.done(ins)
        dve.wait(t)
        dve.eng.wait_ge(core.scattered[j], rounds * 16)
        mt, idx = core.mt[j], core.idx[j]
        t = core.ev["bank read", 7] = dve.done(dve.eng.tensor_copy(mt, core.bank[7][:, 0:4]))
        dve.wait(t)
        t = dve.done(dve.eng.tensor_scalar(mt[:, 3:4], mt[:, 3:4], -4.0 * T, 4.0 * T, ALU.mult, ALU.add))
        dve.wait(t)
        dve.eng.tensor_scalar(idx, mt[:, 0:2], mt[:, 3:4], None, ALU.add).then_inc(core.idx_ready, 1)
        pool.eng.wait_ge(core.idx_ready, 1)
        pool.eng.sem_clear(core.idx_ready)
        pool.eng.indirect_dma_start(core.xg, None, core.hscr, bass.IndirectOffsetOnAxis(ap=idx[:, 0:1].bitcast(U32), axis=0),
                                    bounds_check=T - 1, oob_is_err=False).then_inc(core.gathered, 16)
    return rest


def turn(core, q, block, h):
    pe = core.pe
    if h == 0:
        pe.eng.wait_ge(core.gathered, block * 16 + 16)
    pe.wait(core.ev["bank read", h])
    for k in range(4):
        kk = 4 * h + k
        ins = pe.eng.transpose(core.bank[h][:, k * P:(k + 1) * P], core.xg[:, kk * P:(kk + 1) * P], const(core, "ident"))
    t = pe.done(ins)
    e = (core.act, core.dve)[h]
    e.wait(t, core.ev["xT used", q])
    copy = e.eng.tensor_copy if h else e.eng.copy
    core.ev["bank read", h] = core.ev["xT written", h] = e.done(
        copy(core.xT[q][:, 4 * h:4 * h + 4, :].rearrange("p k t -> p (k t)"), core.bank[h]))


def expert(core, j, block, rounds, nxt, refill=None, prior=None):
    pe, act, dve, pool = core.pe, core.act, core.dve, core.pool
    q, after = j % 2, (j + 1) % SETS
    w, xT = core.w[q], core.xT[q]
    if nxt is not None:
        rest = dispatch(core, after, nxt, 0, rounds + 1 if after == 0 else rounds)

    def product(bank, name):
        pe.wait(core.ev["bank read", bank])
        for h in range(2):
            pe.wait(core.ev["xT written", h])
            w[name, h].wait(pe)
            for k in range(4):
                ins = pe.eng.matmul(core.bank[bank], xT[:, 4 * h + k, :], w[name, h].ap[:, k * EH:(k + 1) * EH],
                                    start=h + k == 0, stop=h == 1 and k == 3)
            t = pe.done(ins)
            if refill is not None:
                load_expert(core, q, (name, h), refill, t)
        return t
    t = product(2, "e1")
    act.wait(t, core.ev["hN turned"])
    t1 = act.done(act.eng.activation(core.sig, core.bank[2], ACT.Exp, scale=-1.0))
    if nxt is not None:
        rest()
    dve.wait(t1)
    dve.wait(dve.done(dve.eng.tensor_scalar(core.sig, core.sig, 1.0, None, ALU.add)))
    dve.wait(dve.done(dve.eng.reciprocal(core.sig, core.sig)))
    t1 = core.ev["bank read", 2] = dve.done(dve.eng.tensor_tensor(core.sig, core.sig, core.bank[2], ALU.mult))
    t = core.ev["xT used", q] = product(3, "e3")
    dve.wait(t, t1)
    th = core.ev["bank read", 3] = dve.done(dve.eng.tensor_tensor(core.hN, core.sig, core.bank[3], ALU.mult))
    if nxt is not None:
        turn(core, 1 - q, block + 1, 0)
    pe.wait(th, core.ev["bank read", 4])
    for k in range(EH // P):
        ins = pe.eng.transpose(core.bank[4][:, k * P:(k + 1) * P], core.hN[:, k * P:(k + 1) * P], const(core, "ident"))
    t = core.ev["hN turned"] = pe.done(ins)
    act.wait(t, core.ev["hT used"])
    t = core.ev["bank read", 4] = act.done(act.eng.copy(core.hT.rearrange("p k t -> p (k t)"), core.bank[4]))
    if nxt is not None:
        turn(core, 1 - q, block + 1, 1)
    pe.wait(t)
    for h in range(2):
        w["e2", h].wait(pe)
        for k in range(2):
            for n in range(2):
                ins = pe.eng.matmul(core.bank[5 + n], core.hT[:, 2 * h + k, :], w["e2", h].ap[:, k * D + n * T:k * D + (n + 1) * T],
                                    start=h + k == 0, stop=h == 1 and k == 1)
        t = pe.done(ins)
        if refill is not None:
            load_expert(core, q, ("e2", h), refill, t)
    core.ev["hT used"] = t
    gate, o = core.mt[j][:, 2:3], core.oN[j]
    act.wait(t, prior)
    act.eng.wait_ge(core.scattered[j], rounds * 16)
    act.eng.activation(o[:, 0:T], core.bank[5], ACT.Copy, scale=gate).then_inc(core.o_ready, 1)
    dve.wait(t, prior)
    dve.eng.wait_ge(core.scattered[j], rounds * 16)
    dve.eng.tensor_scalar(o[:, T:], core.bank[6], gate, None, ALU.mult).then_inc(core.o_ready, 1)
    pool.eng.wait_ge(core.o_ready, 2)
    pool.eng.sem_clear(core.o_ready)
    pool.eng.indirect_dma_start(core.yscr, bass.IndirectOffsetOnAxis(ap=core.idx[j][:, 1:2].bitcast(U32), axis=0), o, None,
                                bounds_check=2 * T - 1, oob_is_err=False).then_inc(core.scattered[j], 16)


def add_choices(core):
    pe, act, dve, sp = core.pe, core.act, core.dve, core.sp
    pairs = [Landing(core.u[:, 4 * q:4 * q + 4, :].rearrange("p k t -> p (k t)"), sem(core, f"pairs{q}")) for q in range(2)]
    outs = [core.oN[q] for q in range(2)]
    out_sem = [sem(core, f"out{q}") for q in range(2)]
    y = core.yscr.rearrange("(t c) d -> t (c d)", c=2)
    used = [None, None]
    for b in range(NB):
        q = b % 2
        pairs[q].load(sp, y[b * P:(b + 1) * P, :], used[q])
        pr = pairs[q].ap
        pairs[q].wait(dve)
        if b >= 2:
            dve.eng.wait_ge(out_sem[q], 16)
        t = dve.done(dve.eng.tensor_tensor(outs[q], pr[:, 0:D], pr[:, D:], ALU.add))
        used[q] = t
        dve.wait(t)
        for h in range(2):
            bank = 2 * q + h
            pe.wait(core.ev["bank read", bank])
            for k in range(4):
                ins = pe.eng.transpose(core.bank[bank][:, k * P:(k + 1) * P], core.x[:, 4 * h + k, b * P:(b + 1) * P], const(core, "ident"))
            dve.wait(pe.done(ins))
            o = outs[q][:, h * T:(h + 1) * T]
            t = core.ev["bank read", bank] = dve.done(dve.eng.tensor_tensor(o, o, core.bank[bank], ALU.add))
        act.wait(t)
        act.eng.dma_start(core.out[b * P:(b + 1) * P, :], outs[q]).then_inc(out_sem[q], 16)
    for q in range(2):
        sp.eng.wait_ge(out_sem[q], 32)


def kernel(**inputs):
    import concourse.bacc as bacc
    from concourse.bass_utils import run_bass_kernel_spmd

    arrays, vpack = lay_out({n: np.asarray(a) for n, a in inputs.items()})
    cpack = Packed(shape_constants())
    arrays["consts"], arrays["vecs"] = cpack.array, vpack.array
    arrays = {n: np.ascontiguousarray(a) for n, a in arrays.items()}
    nc = bacc.Bacc("TRN2", target_bir_lowering=False, num_devices=1)
    t = {n: nc.dram_tensor("in_" + n, a.shape, mybir.dt.from_np(a.dtype), kind="ExternalInput").ap() for n, a in arrays.items()}
    out = nc.dram_tensor("out", [T, D], F32, kind="ExternalOutput").ap()
    program(nc, t, cpack, vpack, out)
    r = run_bass_kernel_spmd(nc, [{"in_" + n: a for n, a in arrays.items()}], core_ids=[0])
    return r.results[0]["out"].reshape(1, T, D)
```
